# Optimizing a Trainium2 kernel written in Bass

```python
import jax, jax.numpy as jnp
from jax import lax
import numpy as np

D_MODEL = 1024
BATCH = 1
SEQ = 256
DEPTH = 2

HEAD_DIM = 64
HEADS_PER_GROUP = 4
ATTN_GROUPS = ((128, 1), (512, 4), (2048, 16))
N_GROUPS = len(ATTN_GROUPS)
ATTN_HEADS = HEADS_PER_GROUP * N_GROUPS
QKV_W = ATTN_HEADS * HEAD_DIM
ATTN_OUT_W = HEADS_PER_GROUP * HEAD_DIM
CONV_W = D_MODEL
CONV_K = 31
D_FF = 2816
ROPE_THETA = 10000.0
EPS = 1e-6
N_BRANCH = 2
N_IN = 3 * QKV_W + 2 * CONV_W + N_BRANCH * D_MODEL
SPLITS = (QKV_W, 2 * QKV_W, 3 * QKV_W, 3 * QKV_W + 2 * CONV_W)
N_MOD = 9
NEG_INF = -1e30

kernel_name = "hybrid_dilated_attn_conformer_conv_macaron"

def rms_norm(x, g):
    xf = x.astype(jnp.float32)
    y = xf * lax.rsqrt(jnp.mean(xf * xf, axis=-1, keepdims=True) + EPS)
    return (y * g.astype(jnp.float32)).astype(x.dtype)

def layer_norm(x, g, b):
    xf = x.astype(jnp.float32)
    mu = jnp.mean(xf, axis=-1, keepdims=True)
    xc = xf - mu
    var = jnp.mean(xc * xc, axis=-1, keepdims=True)
    return (xc * lax.rsqrt(var + EPS) * g.astype(jnp.float32) + b.astype(jnp.float32)).astype(x.dtype)

def rope_tables(s):
    half = HEAD_DIM // 2
    inv_freq = ROPE_THETA ** (-(jnp.arange(half, dtype=jnp.float32) * 2.0 / HEAD_DIM))
    ang = jnp.arange(s, dtype=jnp.float32)[:, None] * inv_freq[None, :]
    return jnp.cos(ang), jnp.sin(ang)

def apply_rope(t, cos, sin):
    half = HEAD_DIM // 2
    tf = t.astype(jnp.float32)
    t1, t2 = tf[..., :half], tf[..., half:]
    c = cos[None, :, None, :]
    s = sin[None, :, None, :]
    return jnp.concatenate([t1 * c - t2 * s, t2 * c + t1 * s], axis=-1).astype(t.dtype)

def dilated_window_attention(q, k, v, window, dilation):
    b, s, h, e = q.shape
    w = window // dilation
    sp = -(-s // window) * window
    pad = sp - s
    nb = sp // window
    seg = sp // dilation

    def to_blocks(t):
        t = jnp.pad(t, ((0, 0), (0, pad), (0, 0), (0, 0)))
        t = t.reshape(b, seg, dilation, h, e).transpose(0, 2, 1, 3, 4)
        return t.reshape(b, dilation, nb, w, h, e)

    def with_prev(t):
        prev = jnp.pad(t, ((0, 0), (0, 0), (1, 0), (0, 0), (0, 0), (0, 0)))[:, :, :-1]
        return jnp.concatenate([prev, t], axis=3)

    qb = to_blocks(q)
    kk = with_prev(to_blocks(k))
    vv = with_prev(to_blocks(v))

    scores = jnp.einsum('bdnqhe,bdnkhe->bdnhqk', qb, kk,
                        preferred_element_type=jnp.float32) * (e ** -0.5)
    qi = jnp.arange(w)[:, None]
    kj = jnp.arange(2 * w)[None, :]
    dist = qi + w - kj
    band = (dist >= 0) & (dist <= w)
    has_prev = (jnp.arange(nb)[:, None, None] > 0) | (kj[None] >= w)
    mask = (band[None] & has_prev)[:, None]
    scores = jnp.where(mask, scores, NEG_INF)
    m = jnp.max(scores, axis=-1, keepdims=True)
    p = jnp.exp(scores - m)
    den = jnp.sum(p, axis=-1)
    o = jnp.einsum('bdnhqk,bdnkhe->bdnqhe', p, vv.astype(jnp.float32))
    o = o / jnp.transpose(den, (0, 1, 2, 4, 3))[..., None]
    lse = m[..., 0] + jnp.log(den)

    o = o.reshape(b, dilation, seg, h, e).transpose(0, 2, 1, 3, 4).reshape(b, sp, h, e)[:, :s]
    lse = jnp.transpose(lse, (0, 1, 2, 4, 3)).reshape(b, dilation, seg, h)
    lse = lse.transpose(0, 2, 1, 3).reshape(b, sp, h)[:, :s]
    return o, lse

def conv_module(u, conv_w, conv_b, ln_g, ln_b, w_o):
    a, g = jnp.split(u, 2, axis=-1)
    h = a * jax.nn.sigmoid(g)
    h = lax.conv_general_dilated(h, conv_w[:, None, :], window_strides=(1,),
                                 padding=[(CONV_K - 1, 0)],
                                 dimension_numbers=('NWC', 'WIO', 'NWC'),
                                 feature_group_count=CONV_W) + conv_b
    h = jax.nn.silu(layer_norm(h, ln_g, ln_b))
    return h @ w_o

def swiglu(h, wg, wu, wd):
    return (jax.nn.silu(h @ wg) * (h @ wu)) @ wd

def setup_inputs(seed: int = 0) -> dict:
    key = jax.random.key(seed)
    ks = jax.random.split(key, 20)
    f32 = jnp.float32
    nrm = lambda k, shape, scale: (jax.random.normal(k, shape, f32) * scale)
    return {
        "x": nrm(ks[0], (BATCH, SEQ, D_MODEL), 1.0),
        "c": nrm(ks[1], (BATCH, D_MODEL), 1.0),
        "ada_w": nrm(ks[2], (DEPTH, D_MODEL, N_MOD * D_MODEL), 0.5 * D_MODEL ** -0.5),
        "ada_b": nrm(ks[3], (DEPTH, N_MOD * D_MODEL), 0.02),
        "norm_g": 1.0 + nrm(ks[4], (DEPTH, 3, D_MODEL), 0.02),
        "ffn_wg": nrm(ks[5], (DEPTH, 2, D_MODEL, D_FF), D_MODEL ** -0.5),
        "ffn_wu": nrm(ks[6], (DEPTH, 2, D_MODEL, D_FF), D_MODEL ** -0.5),
        "ffn_wd": nrm(ks[7], (DEPTH, 2, D_FF, D_MODEL), D_FF ** -0.5),
        "w_in": nrm(ks[8], (DEPTH, D_MODEL, N_IN), D_MODEL ** -0.5),
        "attn_wo": nrm(ks[9], (DEPTH, ATTN_OUT_W, D_MODEL), ATTN_OUT_W ** -0.5),
        "conv_w": nrm(ks[10], (DEPTH, CONV_K, CONV_W), CONV_K ** -0.5),
        "conv_b": nrm(ks[11], (DEPTH, CONV_W), 0.02),
        "conv_ln_g": 1.0 + nrm(ks[12], (DEPTH, CONV_W), 0.02),
        "conv_ln_b": nrm(ks[13], (DEPTH, CONV_W), 0.02),
        "conv_wo": nrm(ks[14], (DEPTH, CONV_W, D_MODEL), CONV_W ** -0.5),
        "w_out": nrm(ks[15], (DEPTH, D_MODEL, D_MODEL), D_MODEL ** -0.5),
        "final_g": 1.0 + nrm(ks[16], (D_MODEL,), 0.02),
    }

def reference(x, c, ada_w, ada_b, norm_g, ffn_wg, ffn_wu, ffn_wd, w_in, attn_wo,
              conv_w, conv_b, conv_ln_g, conv_ln_b, conv_wo, w_out, final_g):
    b, s, d = x.shape
    cos, sin = rope_tables(s)
    c_act = jax.nn.silu(c)
    for l in range(DEPTH):
        mod = (c_act @ ada_w[l] + ada_b[l]).reshape(b, N_MOD, d)[:, :, None, :]
        shift = lambda i: mod[:, 3 * i]
        scale = lambda i: mod[:, 3 * i + 1]
        gate = lambda i: mod[:, 3 * i + 2]
        modulate = lambda t, i: rms_norm(t, norm_g[l, i]) * (1.0 + scale(i)) + shift(i)

        h = modulate(x, 0)
        x = x + 0.5 * gate(0) * swiglu(h, ffn_wg[l, 0], ffn_wu[l, 0], ffn_wd[l, 0])

        h = modulate(x, 1)
        z = h @ w_in[l]
        q, k, v, u, gates = jnp.split(z, SPLITS, axis=-1)
        q = apply_rope(q.reshape(b, s, ATTN_HEADS, HEAD_DIM), cos, sin)
        k = apply_rope(k.reshape(b, s, ATTN_HEADS, HEAD_DIM), cos, sin)
        v = v.reshape(b, s, ATTN_HEADS, HEAD_DIM)
        outs, lses = [], []
        for g_idx, (win, dil) in enumerate(ATTN_GROUPS):
            sl = slice(g_idx * HEADS_PER_GROUP, (g_idx + 1) * HEADS_PER_GROUP)
            o_g, lse_g = dilated_window_attention(q[:, :, sl], k[:, :, sl], v[:, :, sl], win, dil)
            outs.append(o_g)
            lses.append(lse_g)
        wts = jax.nn.softmax(jnp.stack(lses, axis=0), axis=0)
        o = jnp.sum(wts[..., None] * jnp.stack(outs, axis=0), axis=0)
        y_attn = o.astype(x.dtype).reshape(b, s, ATTN_OUT_W) @ attn_wo[l]
        y_conv = conv_module(u, conv_w[l], conv_b[l], conv_ln_g[l], conv_ln_b[l], conv_wo[l])
        g_attn, g_conv = jnp.split(gates, N_BRANCH, axis=-1)
        y = jax.nn.sigmoid(g_attn) * y_attn + jax.nn.sigmoid(g_conv) * y_conv
        x = x + gate(1) * (y @ w_out[l])

        h = modulate(x, 2)
        x = x + 0.5 * gate(2) * swiglu(h, ffn_wg[l, 1], ffn_wu[l, 1], ffn_wd[l, 1])
    return rms_norm(x, final_g)


_drawn_inputs = setup_inputs


def setup_inputs(seed=0):
    import zlib

    import numpy as np

    out = dict(_drawn_inputs(seed))
    spreads = {}
    factors = {'ada_b': 2.75,
     'norm_g': 7.876,
     'conv_b': 29.986,
     'conv_ln_g': 57.306,
     'conv_ln_b': 51.159,
     'final_g': 8.21}
    for name, (base, spread) in spreads.items():
        noise = np.random.default_rng([zlib.crc32(name.encode()), seed]).standard_normal(out[name].shape)
        drawn = base * np.exp(spread * noise) if base else spread * noise
        out[name] = __import__('jax').numpy.asarray(drawn.astype(out[name].dtype))
    for name, factor in factors.items():
        out[name] = (out[name] * factor).astype(out[name].dtype)
    return out
```

```python
from contextlib import ExitStack

import concourse.bass as bass
from concourse import mybir

ALU = mybir.AluOpType
ACT = mybir.ActivationFunctionType
AX = mybir.AxisListType
F32 = mybir.dt.float32
F32R = mybir.dt.float32r
BF16 = mybir.dt.bfloat16

P = 128
D = 1024
T = 256
DEPTH = 2
KC = D // P
TT = T // P
FF = 2816
FB = FF // 256
HD = 64
HPG = 4
NG = 3
DILATION = (1, 4, 16)
WINDOW = (128, 512, 2048)
TAPS = 31
PAD = TAPS - 1
GROUPS = 3 * DEPTH
GW = 3 * D
EPS = 1e-6
PW = KC * 256
RING = 3

FFN_PANELS = 3 * FB
M_U, M_QK, M_GA0, M_V, M_G, M_AO, M_CO, M_WO = 0, 8, 14, 15, 18, 25, 26, 30
MIX_PANELS = 34
LAYER_PANELS = 2 * FFN_PANELS + MIX_PANELS
PANELS = DEPTH * LAYER_PANELS

C_C = 0
C_FG = C_C + KC
C_LAYER = C_FG + KC
L_ADAB, L_NG, L_CW = 0, 9 * KC, 12 * KC
L_CB = L_CW + TAPS * KC
L_LG, L_LB = L_CB + KC, L_CB + 2 * KC
L_W = L_CB + 3 * KC
NPAR = C_LAYER + DEPTH * L_W


def col(layer, which, n=0):
    return C_LAYER + layer * L_W + which + n


def decoder_program(nc, xT, params, rope, perm, mask, ada_w, ffn_wg, ffn_wu, ffn_wd, w_in, attn_wo, conv_wo, w_out, out):
    with ExitStack() as ctx:
        def sb(name, shape, dt=F32):
            return ctx.enter_context(nc.sbuf_tensor(name, shape, dt))

        def sem(name):
            return ctx.enter_context(nc.semaphore(name))

        raw = sb("raw", [P, RING, PW])
        w_hi = sb("w_hi", [P, RING, PW], F32R)
        w_lo = sb("w_lo", [P, RING, PW], F32R)
        x = sb("x", [P, KC, T])
        work = sb("work", [P, KC, T])
        hA_hi = sb("hA_hi", [P, KC, T], F32R)
        hA_lo = sb("hA_lo", [P, KC, T], F32R)
        hB_hi = sb("hB_hi", [P, KC, T], F32R)
        hB_lo = sb("hB_lo", [P, KC, T], F32R)
        conv_in = sb("conv_in", [P, KC, PAD + T])
        v_sb = sb("v_sb", [P, TT, NG * 256])
        tmp_a = sb("tmp_a", [P, 2, T])
        tmp_b = sb("tmp_b", [P, 2, T])
        mid_hi = sb("mid_hi", [P, 2, T], F32R)
        mid_lo = sb("mid_lo", [P, 2, T], F32R)
        mask_sb = sb("mask_sb", [P, TT, NG, T], BF16)
        rope_sb = sb("rope_sb", [P, 2, T])
        perm_sb = sb("perm_sb", [P, 2, P])
        par = sb("par", [P, NPAR])
        ones = sb("ones", [P, P])
        zeros = sb("zeros", [P, 512], BF16)
        c_act = sb("c_act", [P, KC])
        mods = sb("mods", [P, GROUPS, 3 * KC])
        gs = sb("gs", [P, GROUPS, KC])
        gate = sb("gate", [P, GROUPS, KC])
        std = sb("std", [P, T])
        rstd = sb("rstd", [P, T])
        eps = sb("eps", [P, 1])
        rowmax = sb("rowmax", [P, 2 * HPG])
        negmax = sb("negmax", [P, 2 * HPG])
        den = sb("den", [P, 2 * HPG])
        rden = sb("rden", [P, 2 * HPG])
        arena = sb("arena", [P, 4 * GW])
        ada_raw = [arena[:, i * GW:(i + 1) * GW] for i in range(2)]
        ada_acc = [arena[:, (2 + i) * GW:(3 + i) * GW] for i in range(2)]
        gates = arena[:, 0:16 * T].rearrange("p (c t) -> p c t", t=T)
        y_attn = arena[:, 16 * T:24 * T].rearrange("p (c t) -> p c t", t=T)
        o = 24 * T
        qk = arena[:, o:o + 12 * T].rearrange("p (g w c t) -> p g w c t", g=NG, w=2, t=T)
        o += 12 * T
        probs = [arena[:, o + 3 * T:o + 3 * T + 3 * P].rearrange("p (g t) -> p g t", g=NG),
                 arena[:, o:o + 3 * T].rearrange("p (g t) -> p g t", g=NG)]
        o += 3 * T + 3 * P
        probsT = arena[:, o:o + 6 * T].rearrange("p (g k t) -> p g k t", g=NG, k=TT)
        assert o + 6 * T <= 4 * GW

        ps = ctx.enter_context(nc.psum_tensor("ps", [P, 8, 512], F32))
        B_G, B_U, B_STAT, B_ADA = 4, 5, 6, 7
        KBANK = (3, 4, 5)
        S1 = ps[:, 0:2, :].rearrange("p b n -> p (b n)")[:, 0:NG * T].rearrange("p (g t) -> p g t", g=NG)
        S0 = ps[:, 2, 0:NG * P].rearrange("p (g t) -> p g t", g=NG)
        T1 = ps[:, 0:2, :].rearrange("p b n -> p (b n)")[:, 0:6 * P].rearrange("p (g k t) -> p g k t", g=NG, k=TT)
        T0 = S0

        def pair(bank):
            return ps[:, bank, :].rearrange("p (c t) -> p c t", t=T)

        def acc(o):
            return ps[:, o // 2, (o % 2) * T:(o % 2 + 1) * T]

        consts_in = sem("consts_in")
        tables_in = sem("tables_in")
        raw_in = [sem(f"raw_in{i}") for i in range(RING)]
        ada_in = [sem(f"ada_in{i}") for i in range(2)]
        out_done = sem("out_done")
        setup_done = sem("setup_done")
        c_ready = sem("c_ready")
        hi_done, lo_done, panel_done = sem("hi_done"), sem("lo_done"), sem("panel_done")
        ada_step, ada_cols, mods_done, mods_step = sem("ada_step"), sem("ada_cols"), sem("mods_done"), sem("mods_step")
        sq_done, ssq_done, std_done, rstd_done = sem("sq_done"), sem("ssq_done"), sem("std_done"), sem("rstd_done")
        t_done, h_hi_done, h_lo_done = sem("t_done"), sem("h_hi_done"), sem("h_lo_done")
        silu_done, mid_done, mid_hi_done, mid_lo_done = sem("silu_done"), sem("mid_done"), sem("mid_hi_done"), sem("mid_lo_done")
        acc_done, x_done = sem("acc_done"), sem("x_done")
        evac_done, glu_done, conv_step = sem("evac_done"), sem("glu_done"), sem("conv_step")
        rot_done, rope_mul, rope_done = sem("rot_done"), sem("rope_mul"), sem("rope_done")
        score_done, masked_done, max_done, exp_done = sem("score_done"), sem("masked_done"), sem("max_done"), sem("exp_done")
        rden_done, prob_done, turn_done, probT_done = sem("rden_done"), sem("prob_done"), sem("turn_done"), sem("probT_done")
        pv_done, o_hi_done, o_lo_done = sem("pv_done"), sem("o_hi_done"), sem("o_lo_done")
        gates_done = sem("gates_done")
        ln_sum, xc_done, ln_sq, ln_std, ln_rstd = sem("ln_sum"), sem("xc_done"), sem("ln_sq"), sem("ln_std"), sem("ln_rstd")
        ln_t, ln_silu, ln_hi, ln_lo = sem("ln_t"), sem("ln_silu"), sem("ln_hi"), sem("ln_lo")
        ao_done, ya_done, yc_done, y_done, y_hi_done, y_lo_done = (
            sem("ao_done"), sem("ya_done"), sem("yc_done"), sem("y_done"), sem("y_hi_done"), sem("y_lo_done"))
        final_done = sem("final_done")
        cleared = sem("cleared")
        gate_done = sem("gate_done")

        wg_v = ffn_wg.rearrange("l f (k p) n -> l f p k n", p=P)
        wu_v = ffn_wu.rearrange("l f (k p) n -> l f p k n", p=P)
        wd_v = ffn_wd.rearrange("l f (j k p) n -> l f j p k n", k=2, p=P)
        win_v = w_in.rearrange("l (k p) n -> l p k n", p=P)
        ao_v = attn_wo.rearrange("l (k p) n -> l p k n", p=P)
        co_v = conv_wo.rearrange("l (k p) n -> l p k n", p=P)
        wo_v = w_out.rearrange("l (k p) n -> l p k n", p=P)

        def kview(flat):
            return flat.rearrange("p (k n) -> p k n", k=KC)

        def dview(flat):
            return flat.rearrange("p (k n) -> p k n", k=2)

        QKV = NG * 256
        U0, GA0 = 3 * QKV, 3 * QKV + 2 * D
        win_cols = []
        for i in range(4):
            win_cols += [U0 + 256 * i, U0 + D + 256 * i]
        for g in range(NG):
            win_cols += [256 * g, QKV + 256 * g]
        win_cols += [GA0]
        win_cols += [2 * QKV + 256 * g for g in range(NG)]
        win_cols += [GA0 + 256 * i for i in range(1, 8)]

        def ffn_base(f):
            return (f // 2) * LAYER_PANELS + (f % 2) * (FFN_PANELS + MIX_PANELS)

        def mix_base(l):
            return l * LAYER_PANELS + FFN_PANELS

        def ada_before(f):
            return 2 * KC + (f // 2) * 3 * KC + (f % 2) * 2 * KC

        def ada_groups(f):
            g = 3 * (f // 2) + (1 if f % 2 == 0 else 3)
            return [g, g + 1] if f % 2 == 0 else ([g] if g < GROUPS else [])

        def prod_end(f):
            return min(ffn_base(f) + FFN_PANELS + 2, PANELS)

        block = ctx.enter_context(nc.Block())

        @block.sync
        def _(sp):
            def load(p, dst_view, src):
                slot = p % RING
                if p >= RING:
                    sp.wait_ge(lo_done, p - RING + 1)
                sp.dma_start(dst_view(raw[:, slot, :]), src).then_inc(raw_in[slot], 16)

            sp.dma_start(par[:], params).then_inc(consts_in, 16)
            sp.dma_start(x[:], xT).then_inc(consts_in, 16)
            sp.dma_start(rope_sb[:], rope).then_inc(tables_in, 16)
            sp.dma_start(perm_sb[:], perm).then_inc(tables_in, 16)
            sp.dma_start(mask_sb[:], mask).then_inc(tables_in, 16)

            def ffn(f):
                l, s = f // 2, f % 2
                base = ffn_base(f)
                load(base, kview, wg_v[l, s, :, :, 0:256])
                load(base + 1, kview, wu_v[l, s, :, :, 0:256])
                with sp.Fori(0, FB - 1) as j:
                    p = base + 2
                    for i, (view, src) in enumerate((
                            (kview, wg_v[l, s, :, :, bass.ds(j * 256 + 256, 256)]),
                            (kview, wu_v[l, s, :, :, bass.ds(j * 256 + 256, 256)]),
                            (dview, wd_v[l, s, bass.ds(j, 1)].rearrange("o p k n -> (o p) k n")))):
                        slot = (p + i) % RING
                        sp.wait_ge(lo_done, j * 3 + (p + i - RING + 1))
                        sp.dma_start(view(raw[:, slot, :]), src).then_inc(raw_in[slot], 16)
                load(base + FFN_PANELS - 1, dview, wd_v[l, s, FB - 1])

            def mix(l):
                base = mix_base(l)
                for i, c in enumerate(win_cols):
                    load(base + i, kview, win_v[l, :, :, c:c + 256])
                load(base + M_AO, dview, ao_v[l])
                for i in range(4):
                    load(base + M_CO + i, kview, co_v[l, :, :, 256 * i:256 * i + 256])
                for i in range(4):
                    load(base + M_WO + i, kview, wo_v[l, :, :, 256 * i:256 * i + 256])

            for l in range(DEPTH):
                ffn(2 * l)
                mix(l)
                ffn(2 * l + 1)
            for k in range(KC):
                sp.wait_ge(final_done, k + 1)
                sp.dma_start(out[:, k, :], work[:, k, :]).then_inc(out_done, 16)
            sp.wait_ge(out_done, 16 * KC)

        @block.gpsimd
        def _(pool):
            for n in range(2 * KC):
                if n >= 2:
                    pool.wait_ge(ada_step, n - 1)
                a, b = (0, 2 * D) if n < KC else (2 * D, GW)
                pool.dma_start(ada_raw[n % 2][:, a:b], ada_w[0, (n % KC) * P:(n % KC + 1) * P, a:b]).then_inc(ada_in[n % 2], 16)
            for f in range(2 * DEPTH):
                groups = ada_groups(f)
                if not groups:
                    continue
                if f % 2 == 1:
                    pool.wait_ge(x_done, KC * (3 * (f // 2) + 2))
                elif f > 0:
                    pool.wait_ge(ada_step, ada_before(f))
                with pool.Fori(0, KC) as j:
                    for i, g in enumerate(groups):
                        pool.wait_ge(ada_step, j * len(groups) + (ada_before(f) + (i - 1 if len(groups) == 2 else 0)))
                        src = ada_w[g // 3].rearrange("(k p) n -> k p n", p=P)[bass.ds(j, 1), :,
                                                                               (g % 3) * GW:(g % 3 + 1) * GW]
                        pool.dma_start(ada_raw[i], src.rearrange("o p n -> (o p) n")).then_inc(ada_in[i], 16)

        @block.tensor
        def _(pe):
            def three(out_ap, stat, mov, start, stop, **kw):
                nc.tensor.matmul(out_ap, stat[0], mov[0], start=start, stop=False, **kw)
                nc.tensor.matmul(out_ap, stat[0], mov[1], start=False, stop=False, **kw)
                return nc.tensor.matmul(out_ap, stat[1], mov[0], start=False, stop=stop, **kw)

            def k_panel(slot, rhs, bank, h_wait=None):
                hi, lo = kview(w_hi[:, slot, :]), kview(w_lo[:, slot, :])
                for t in range(2):
                    c = slice(t * P, (t + 1) * P)
                    for k in range(KC):
                        if t == 0 and h_wait is not None:
                            h_wait(k)
                        mm = three(pair(bank)[:, t, :], (hi[:, k, c], lo[:, k, c]),
                                   (rhs[0][:, k, :], rhs[1][:, k, :]), k == 0, k == KC - 1)
                mm.then_inc(panel_done, 1)

            def split_ready(p):
                pe.wait_ge(hi_done, p + 1)
                pe.wait_ge(lo_done, p + 1)

            hA = (hA_hi, hA_lo)
            hB = (hB_hi, hB_lo)

            def column_sums(n_sem, done_sem, base, src):
                for k in range(KC):
                    pe.wait_ge(n_sem, base + k + 1)
                    mm = nc.tensor.matmul(ps[:, B_STAT, 0:T], ones[:], src(k), start=(k == 0), stop=(k == KC - 1))
                mm.then_inc(done_sem, 1)

            def norm(n):
                column_sums(sq_done, ssq_done, KC * n, lambda k: work[:, k, :])

            def ada_columns(n, f_units, which, first=0, last=3 * KC):
                pe.wait_ge(ada_step, f_units)
                if n > 0:
                    pe.wait_ge(mods_step, n)
                for c in range(first, last):
                    mm = nc.tensor.matmul(ps[:, B_ADA, c:c + 1], ada_acc[which][:, c * P:(c + 1) * P], ones[:, 0:1],
                                          start=True, stop=True)
                mm.then_inc(ada_cols, 1)

            def d_panel(slot, j_last=False):
                hi, lo = dview(w_hi[:, slot, :]), dview(w_lo[:, slot, :])
                if not j_last:
                    for kk in range(2):
                        for o in range(KC):
                            c = slice(o * P, (o + 1) * P)
                            mm = three(acc(o), (hi[:, kk, c], lo[:, kk, c]), (mid_hi[:, kk, :], mid_lo[:, kk, :]),
                                       False, False, skip_group_check=True)
                    mm.then_inc(panel_done, 1)
                else:
                    for o in range(KC):
                        for kk in range(2):
                            c = slice(o * P, (o + 1) * P)
                            mm = three(acc(o), (hi[:, kk, c], lo[:, kk, c]), (mid_hi[:, kk, :], mid_lo[:, kk, :]),
                                       False, kk == 1, skip_group_check=True)
                        if o % 2 == 1:
                            mm.then_inc(acc_done if o < KC - 1 else panel_done, 1)

            def ffn(f):
                base = ffn_base(f)
                n = 3 * (f // 2) + 2 * (f % 2)
                if f > 0:
                    pe.wait_ge(x_done, KC * n)
                for b in range(4):
                    nc.tensor.matmul(ps[:, b, :], zeros[:, 0:P], zeros[:, :], start=True, stop=False,
                                     skip_group_check=True)
                norm(n)
                split_ready(base)
                k_panel(base % RING, hA, B_G, lambda k: pe.wait_ge(h_lo_done, KC * n + k + 1))
                split_ready(base + 1)
                k_panel((base + 1) % RING, hA, B_U)
                if f == 0:
                    ada_columns(1, 2 * KC, 0, 2 * KC)
                with pe.Fori(0, FB - 1) as j:
                    p = base + 2
                    pe.wait_ge(hi_done, j * 3 + (p + 1))
                    pe.wait_ge(lo_done, j * 3 + (p + 1))
                    pe.wait_ge(mid_done, j + (f * FB + 1))
                    k_panel(p % RING, hA, B_G)
                    pe.wait_ge(hi_done, j * 3 + (p + 2))
                    pe.wait_ge(lo_done, j * 3 + (p + 2))
                    k_panel((p + 1) % RING, hA, B_U)
                    pe.wait_ge(hi_done, j * 3 + (p + 3))
                    pe.wait_ge(lo_done, j * 3 + (p + 3))
                    pe.wait_ge(mid_lo_done, j + (f * FB + 1))
                    d_panel((p + 2) % RING)
                for i, g in enumerate(ada_groups(f)):
                    ada_columns(g + 1, ada_before(f) + KC * len(ada_groups(f)), i)
                split_ready(base + FFN_PANELS - 1)
                pe.wait_ge(mid_lo_done, f * FB + FB)
                d_panel((base + FFN_PANELS - 1) % RING, True)

            def mix(l):
                base = mix_base(l)
                e0 = 25 * l
                norm(3 * l + 1)
                pe.wait_ge(h_lo_done, KC * (3 * l + 2))
                first = base

                for i in range(RING):
                    split_ready(first + i)
                    k_panel((first + i) % RING, hA, KBANK[(first + i) % RING])
                with pe.Fori(0, 4) as j:
                    for i in range(RING):
                        q = first + RING + i
                        pe.wait_ge(hi_done, j * RING + (q + 1))
                        pe.wait_ge(lo_done, j * RING + (q + 1))
                        pe.wait_ge(evac_done, j * RING + (e0 + i + 1))
                        k_panel(q % RING, hA, KBANK[q % RING])

                def v_panel(g):
                    p = base + M_V + g
                    slot = p % RING
                    split_ready(p)
                    pe.wait_ge(evac_done, e0 + M_V + g - RING + 1)
                    hi, lo = kview(w_hi[:, slot, :]), kview(w_lo[:, slot, :])
                    for t in range(TT):
                        c = slice(t * P, (t + 1) * P)
                        for k in range(KC):
                            mm = three(pair(KBANK[slot])[:, t, :], (hA_hi[:, k, c], hA_lo[:, k, c]),
                                       (hi[:, k, :], lo[:, k, :]), k == 0, k == KC - 1)
                    mm.then_inc(panel_done, 1)

                pe.wait_ge(tables_in, 48)

                def rotate(g):
                    for w in range(2):
                        r = 6 * l + 2 * g + w
                        pe.wait_ge(evac_done, e0 + M_QK + 2 * g + w + 1)
                        if r % 6 >= 2:
                            pe.wait_ge(rope_done, r - 1)
                        for c in range(2):
                            mm = nc.tensor.matmul(pair((2, 7)[w])[:, c, :], perm_sb[:, 0, :], qk[:, g, w, c, :],
                                                  start=True, stop=True)
                        mm.then_inc(rot_done, 1)

                for g in range(NG):
                    v_panel(g)
                    rotate(g)

                def gate_panel(i):
                    p = base + M_G + i
                    split_ready(p)
                    pe.wait_ge(evac_done, e0 + M_G + i - RING + 1)
                    k_panel(p % RING, hA, KBANK[p % RING])

                def scores(h):
                    if h == 0:
                        pe.wait_ge(rope_done, 6 * (l + 1))
                    else:
                        pe.wait_ge(probT_done, 2 * (HPG * l + h))
                    for q in range(TT):
                        keys = (q + 1) * P
                        for g in range(NG):
                            head = HPG * g + h
                            part = slice((head % 2) * HD, (head % 2 + 1) * HD)
                            c = (head // 2) % 2
                            dst = S1[:, g, :] if q else S0[:, g, :]
                            mm = nc.tensor.matmul(dst, qk[part, g, 0, c, q * P:(q + 1) * P], qk[part, g, 1, c, 0:keys],
                                                  start=True, stop=True)
                        mm.then_inc(score_done, 1)

                def turn(h):
                    for q in range(TT):
                        pe.wait_ge(prob_done, 2 * (HPG * l + h) + q + 1)
                        for g in range(NG):
                            for k in range(q + 1):
                                dst = T1[:, g, k, :] if q else T0[:, g, :]
                                mm = nc.tensor.transpose(dst, probs[q][:, g, k * P:(k + 1) * P], perm_sb[:, 1, :])
                        mm.then_inc(turn_done, 1)

                def pv(h):
                    pe.wait_ge(probT_done, 2 * (HPG * l + h + 1))
                    half = slice((h % 2) * HD, (h % 2 + 1) * HD)
                    bank = 6 + h // 2
                    for g in range(NG):
                        cols = slice((HPG * g + h) * HD, (HPG * g + h + 1) * HD)
                        nc.tensor.matmul(ps[half, bank, 0:T], v_sb[:, 0, cols], probsT[:, g, 0, :],
                                         start=(g == 0), stop=False)
                        mm = nc.tensor.matmul(ps[half, bank, P:T], v_sb[:, 1, cols], probsT[:, g, 1, P:T],
                                              start=False, stop=(g == NG - 1))
                    mm.then_inc(pv_done, 1)

                gate_panel(0)
                scores(0)
                gate_panel(1)
                turn(0)
                gate_panel(2)
                pv(0)
                scores(1)
                gate_panel(3)
                turn(1)
                gate_panel(4)
                pv(1)
                scores(2)
                gate_panel(5)
                turn(2)
                gate_panel(6)
                pv(2)
                scores(3)
                turn(3)
                pv(3)

                p = base + M_AO
                split_ready(p)
                pe.wait_ge(o_lo_done, 2 * (l + 1))
                hi, lo = dview(w_hi[:, p % RING, :]), dview(w_lo[:, p % RING, :])
                for i in range(4):
                    if i == 3:
                        pe.wait_ge(evac_done, e0 + 25)
                    for t in range(2):
                        c = slice((2 * i + t) * P, (2 * i + t + 1) * P)
                        for kk in range(2):
                            mm = three(pair(i)[:, t, :], (hi[:, kk, c], lo[:, kk, c]), (mid_hi[:, kk, :], mid_lo[:, kk, :]),
                                       kk == 0, kk == 1)
                    mm.then_inc(ao_done if i < 3 else panel_done, 1)

                pe.wait_ge(conv_step, KC * TAPS * (l + 1))
                for k in range(KC):
                    mm = nc.tensor.matmul(ps[:, B_STAT, 0:T], ones[:], work[:, k, :], start=(k == 0), stop=(k == KC - 1))
                mm.then_inc(ln_sum, 1)
                pe.wait_ge(xc_done, KC * (l + 1))
                column_sums(ln_sq, ln_sum, KC * l, lambda k: conv_in[:, k, PAD:])

                for i in range(4):
                    p = base + M_CO + i
                    split_ready(p)
                    pe.wait_ge(ya_done, 4 * (l + 1))
                    if i >= 2:
                        pe.wait_ge(yc_done, 4 * l + i - 1)
                    if i == 0:
                        k_panel(p % RING, hA, 4 + i % 2, lambda k: pe.wait_ge(ln_lo, KC * l + k + 1))
                    else:
                        k_panel(p % RING, hA, 4 + i % 2)
                for i in range(4):
                    p = base + M_WO + i
                    split_ready(p)
                    k_panel(p % RING, hB, i, (lambda k: pe.wait_ge(y_lo_done, 4 * l + k // 2 + 1)) if i == 0 else None)

            pe.wait_ge(setup_done, 4)
            ada_columns(0, KC, 0, 0, 2 * KC)
            for l in range(DEPTH):
                ffn(2 * l)
                mix(l)
                ffn(2 * l + 1)
            norm(3 * DEPTH)

        @block.scalar
        def _(act):
            def hi(p):
                slot = p % RING
                act.wait_ge(raw_in[slot], 16 * (p // RING + 1))
                if p >= RING:
                    act.wait_ge(panel_done, p - RING + 1)
                nc.scalar.copy(w_hi[:, slot, :], raw[:, slot, :]).then_inc(hi_done, 1)

            def hi_loop(j, p):
                slot = p % RING
                act.wait_ge(raw_in[slot], j * 16 + 16 * (p // RING + 1))
                act.wait_ge(panel_done, j * 3 + (p - RING + 1))
                nc.scalar.copy(w_hi[:, slot, :], raw[:, slot, :]).then_inc(hi_done, 1)

            def norm(n):
                for k in range(KC):
                    if n > 0:
                        act.wait_ge(x_done, KC * (n - 1) + k + 1)
                    if n == 0 and k == 0:
                        act.wait_ge(consts_in, 32)
                    nc.scalar.activation(work[:, k, :], x[:, k, :], ACT.Square).then_inc(sq_done, 1)
                act.wait_ge(ssq_done, n + 1)
                nc.scalar.activation(std[:], ps[:, B_STAT, 0:T], ACT.Sqrt, bias=eps[:, 0:1],
                                     scale=1.0 / D).then_inc(std_done, 1)
                if n == 3 * DEPTH:
                    return
                for k in range(KC):
                    act.wait_ge(t_done, KC * n + k + 1)
                    nc.scalar.activation(hA_hi[:, k, :], work[:, k, :], ACT.Identity,
                                         bias=mods[:, n, k:k + 1]).then_inc(h_hi_done, 1)

            def silu(f, j):
                nc.scalar.activation(tmp_a[:], pair(B_G), ACT.Silu).then_inc(silu_done, 1)

            def ffn(f):
                base = ffn_base(f)
                norm(3 * (f // 2) + 2 * (f % 2))
                hi(base + 2)
                act.wait_ge(panel_done, base + 1)
                silu(f, 0)
                hi(base + 3)
                hi(base + 4)
                act.wait_ge(mid_done, f * FB + 1)
                nc.scalar.copy(mid_hi[:], tmp_b[:]).then_inc(mid_hi_done, 1)
                last = ffn_base(f) + FFN_PANELS == PANELS
                n = FB - 2 if last else FB - 1
                with act.Fori(0, n) as j:
                    p = base + 2
                    act.wait_ge(panel_done, j * 3 + (p + 1))
                    act.wait_ge(mid_done, j + (f * FB + 1))
                    silu(f, j)
                    hi_loop(j, p + 3)
                    hi_loop(j, p + 4)
                    hi_loop(j, p + 5)
                    act.wait_ge(mid_done, j + (f * FB + 2))
                    nc.scalar.copy(mid_hi[:], tmp_b[:]).then_inc(mid_hi_done, 1)
                if last:
                    p = base + 2 + 3 * n
                    act.wait_ge(panel_done, p + 1)
                    silu(f, n)
                    hi(p + 3)
                    act.wait_ge(panel_done, p + 3)
                    act.wait_ge(mid_done, f * FB + FB)
                    nc.scalar.copy(mid_hi[:], tmp_b[:]).then_inc(mid_hi_done, 1)

            def mix(l):
                base = mix_base(l)
                norm(3 * l + 1)
                hi(base + 2)

                def panel(i, dst, func, src_t=None):
                    act.wait_ge(panel_done, base + i + 1)
                    nc.scalar.activation(dst, pair(KBANK[(base + i) % RING]), func).then_inc(evac_done, 1)
                    hi(base + i + RING)

                for i in range(4):
                    if i:
                        act.wait_ge(glu_done, 4 * l + i)
                    panel(2 * i, tmp_a[:], ACT.Copy)
                    panel(2 * i + 1, tmp_b[:], ACT.Sigmoid)
                for g in range(NG):
                    panel(M_QK + 2 * g, qk[:, g, 0, :, :], ACT.Copy)
                    panel(M_QK + 2 * g + 1, qk[:, g, 1, :, :], ACT.Copy)
                panel(M_GA0, gates[:, 0:2, :], ACT.Copy)
                for g in range(NG):
                    panel(M_V + g, v_sb[:, :, g * 256:(g + 1) * 256], ACT.Copy)

                def gate_panel(i):
                    panel(M_G + i, gates[:, 2 * (i + 1):2 * (i + 2), :], ACT.Copy)

                def exps(h):
                    for q in range(TT):
                        u = 2 * h + q
                        act.wait_ge(max_done, 2 * HPG * l + u + 1)
                        nc.scalar.activation(probs[q], probs[q], ACT.Exp, bias=negmax[:, u:u + 1],
                                             accum_out=den[:, u:u + 1]).then_inc(exp_done, 1)

                def turned(h):
                    if h > 0:
                        act.wait_ge(pv_done, HPG * l + h)
                    act.wait_ge(turn_done, 2 * (HPG * l + h) + 1)
                    nc.scalar.copy(probsT[:, :, 0, 0:P], T0).then_inc(probT_done, 1)
                    act.wait_ge(turn_done, 2 * (HPG * l + h) + 2)
                    nc.scalar.copy(probsT[:, :, :, P:T], T1).then_inc(probT_done, 1)

                def head_out(c):
                    act.wait_ge(pv_done, HPG * l + 2 * c + 2)
                    nc.scalar.copy(mid_hi[:, c, :], ps[:, 6 + c, 0:T]).then_inc(o_hi_done, 1)

                gate_panel(0)
                exps(0)
                gate_panel(1)
                turned(0)
                gate_panel(2)
                exps(1)
                gate_panel(3)
                turned(1)
                gate_panel(4)
                exps(2)
                head_out(0)
                gate_panel(5)
                turned(2)
                gate_panel(6)
                exps(3)
                turned(3)
                head_out(1)
                act.wait_ge(evac_done, 25 * (l + 1))
                nc.scalar.activation(gates[:, 0:8, :], gates[:, 0:8, :], ACT.Sigmoid).then_inc(gates_done, 1)
                nc.scalar.activation(gates[:, 8:16, :], gates[:, 8:16, :], ACT.Sigmoid).then_inc(gates_done, 1)
                hi(base + M_AO + 3)
                for k in range(KC):
                    act.wait_ge(xc_done, KC * l + k + 1)
                    nc.scalar.activation(conv_in[:, k, PAD:], work[:, k, :], ACT.Square).then_inc(ln_sq, 1)
                act.wait_ge(ln_sum, 2 * (l + 1))
                nc.scalar.activation(std[:], ps[:, B_STAT, 0:T], ACT.Sqrt, bias=eps[:, 0:1],
                                     scale=1.0 / D).then_inc(ln_std, 1)
                for k in range(KC):
                    act.wait_ge(ln_t, KC * l + k + 1)
                    nc.scalar.activation(work[:, k, :], conv_in[:, k, PAD:], ACT.Silu,
                                         bias=par[:, col(l, L_LB, k):col(l, L_LB, k) + 1]).then_inc(ln_silu, 1)
                    act.wait_ge(ln_silu, KC * l + k + 1)
                    nc.scalar.copy(hA_hi[:, k, :], work[:, k, :]).then_inc(ln_hi, 1)
                for i in range(4):
                    hi(base + M_CO + i + RING)
                    act.wait_ge(y_done, 4 * l + i + 1)
                    nc.scalar.copy(hB_hi[:, 2 * i:2 * i + 2, :], tmp_b[:]).then_inc(y_hi_done, 1)
                for i in range(3):
                    hi(base + M_WO + i + RING)

            act.wait_ge(consts_in, 32)
            act.wait_ge(setup_done, 4)
            nc.scalar.activation(c_act[:], par[:, C_C:C_C + KC], ACT.Silu).then_inc(c_ready, 1)
            hi(0)
            hi(1)
            for l in range(DEPTH):
                ffn(2 * l)
                mix(l)
                ffn(2 * l + 1)
            norm(3 * DEPTH)

        @block.vector
        def _(dve):
            def split_lo(dst, whole, hi_part):
                return nc.vector.tensor_tensor(dst, whole, hi_part.bitcast(F32), ALU.subtract)

            def lo(p):
                slot = p % RING
                dve.wait_ge(hi_done, p + 1)
                split_lo(w_lo[:, slot, :], raw[:, slot, :], w_hi[:, slot, :]).then_inc(lo_done, 1)

            def lo_loop(j, p):
                slot = p % RING
                dve.wait_ge(hi_done, j * 3 + (p + 1))
                split_lo(w_lo[:, slot, :], raw[:, slot, :], w_hi[:, slot, :]).then_inc(lo_done, 1)

            def recip(n, wait, done):
                dve.wait_ge(wait, n + 1)
                nc.vector.reciprocal(rstd[:], std[:]).then_inc(done, 1)
                dve.wait_ge(done, n + 1)

            def norm(n):
                recip(n, std_done, rstd_done)
                if n == 3 * DEPTH:
                    for k in range(KC):
                        nc.vector.scalar_tensor_tensor(out=work[:, k, :], in0=x[:, k, :],
                                                       scalar=par[:, C_FG + k:C_FG + k + 1], in1=rstd[:],
                                                       op0=ALU.mult, op1=ALU.mult).then_inc(final_done, 1)
                    return
                dve.wait_ge(mods_done, n + 1)
                for k in range(KC + 1):
                    if k < KC:
                        nc.vector.scalar_tensor_tensor(out=work[:, k, :], in0=x[:, k, :], scalar=gs[:, n, k:k + 1],
                                                       in1=rstd[:], op0=ALU.mult, op1=ALU.mult).then_inc(t_done, 1)
                    if k > 0:
                        dve.wait_ge(h_hi_done, KC * n + k)
                        dve.wait_ge(t_done, KC * n + k)
                        nc.vector.scalar_tensor_tensor(out=hA_lo[:, k - 1, :], in0=work[:, k - 1, :],
                                                       scalar=mods[:, n, k - 1:k], in1=hA_hi[:, k - 1, :].bitcast(F32),
                                                       op0=ALU.add, op1=ALU.subtract).then_inc(h_lo_done, 1)

            def add_bias(n, g, first, last):
                dve.wait_ge(ada_cols, n + 1)
                b = col(g // 3, L_ADAB, (g % 3) * 3 * KC)
                nc.vector.tensor_tensor(mods[:, g, first:last], ps[:, B_ADA, first:last], par[:, b + first:b + last],
                                        ALU.add).then_inc(mods_step, 1)
                dve.wait_ge(mods_step, n + 1)

            def finish_gate(g):
                nc.vector.tensor_scalar(gate[:, g, :], mods[:, g, 2 * KC:3 * KC], 1.0 if g % 3 == 1 else 0.5, None,
                                        ALU.mult).then_inc(gate_done, 1)

            def finish_gain(g):
                b = col(g // 3, L_NG, (g % 3) * KC)
                nc.vector.scalar_tensor_tensor(out=gs[:, g, :], in0=mods[:, g, KC:2 * KC], scalar=1.0,
                                               in1=par[:, b:b + KC], op0=ALU.add, op1=ALU.mult).then_inc(mods_done, 1)

            def hidden(f):
                nc.vector.tensor_tensor(tmp_b[:], tmp_a[:], pair(B_U), ALU.mult).then_inc(mid_done, 1)

            def ffn(f):
                base = ffn_base(f)
                n = 3 * (f // 2) + 2 * (f % 2)
                norm(n)
                lo(base + 2)
                if f == 0:
                    first_group(KC, 2 * D, GW)
                lo(base + 3)
                dve.wait_ge(silu_done, f * FB + 1)
                dve.wait_ge(panel_done, base + 2)
                hidden(f)
                lo(base + 4)
                dve.wait_ge(mid_hi_done, f * FB + 1)
                split_lo(mid_lo[:], tmp_b[:], mid_hi[:]).then_inc(mid_lo_done, 1)
                groups = ada_groups(f)
                a0 = ada_before(f)
                if f == 0:
                    add_bias(1, 0, 2 * KC, 3 * KC)
                    finish_gate(0)
                for i in range(len(groups)):
                    nc.vector.memset(ada_acc[i], 0.0).then_inc(cleared, 1)
                if groups:
                    dve.wait_ge(cleared, groups[0] + len(groups))

                def body(j, units):
                    p = base + 2
                    lo_loop(j, p + 3)
                    dve.wait_ge(silu_done, j + (f * FB + 2))
                    dve.wait_ge(panel_done, j * 3 + (p + 2))
                    dve.wait_ge(mid_lo_done, j + (f * FB + 1))
                    hidden(f)
                    lo_loop(j, p + 4)
                    lo_loop(j, p + 5)
                    dve.wait_ge(mid_hi_done, j + (f * FB + 2))
                    split_lo(mid_lo[:], tmp_b[:], mid_hi[:]).then_inc(mid_lo_done, 1)
                    for i in range(units):
                        dve.wait_ge(ada_in[i], j * 16 + ada_dmas(f, i))
                        dve.wait_ge(ada_step, j * units + (a0 + (i - 1 if units == 2 else 0)))
                        nc.vector.scalar_tensor_tensor(out=ada_acc[i], in0=ada_raw[i], scalar=c_act[:, bass.ds(j, 1)],
                                                       in1=ada_acc[i], op0=ALU.mult, op1=ALU.add).then_inc(ada_step, 1)

                last = ffn_base(f) + FFN_PANELS == PANELS
                e = FB - 2 if last else FB - 1
                with dve.Fori(0, KC) as j:
                    body(j, len(groups))
                with dve.Fori(KC, e) as j:
                    body(j, 0)
                if last:
                    p = base + 2 + 3 * e
                    lo(p + 3)
                    dve.wait_ge(silu_done, f * FB + FB)
                    dve.wait_ge(panel_done, p + 2)
                    dve.wait_ge(mid_lo_done, f * FB + FB - 1)
                    hidden(f)
                    dve.wait_ge(mid_hi_done, f * FB + FB)
                    split_lo(mid_lo[:], tmp_b[:], mid_hi[:]).then_inc(mid_lo_done, 1)
                for g in groups:
                    add_bias(g + 1, g, 0, 3 * KC)
                    finish_gain(g)
                    finish_gate(g)
                dve.wait_ge(gate_done, n + 1)
                for i in range(4):
                    if i < 3:
                        dve.wait_ge(acc_done, 3 * f + i + 1)
                    else:
                        dve.wait_ge(panel_done, base + FFN_PANELS)
                    for o in (2 * i, 2 * i + 1):
                        nc.vector.scalar_tensor_tensor(out=x[:, o, :], in0=acc(o), scalar=gate[:, n, o:o + 1],
                                                       in1=x[:, o, :], op0=ALU.mult, op1=ALU.add).then_inc(x_done, 1)

            def ada_dmas(f, slot):
                n = KC
                for e in range(f):
                    n += KC if slot < len(ada_groups(e)) else 0
                return 16 * (n + 1)

            def mix(l):
                base = mix_base(l)
                norm(3 * l + 1)
                lo(base + 2)
                taps_total = KC * TAPS

                def conv(first, last):
                    for s in range(first, min(last, taps_total)):
                        pr, r = divmod(s, 2 * TAPS)
                        t, c = r // 2, 2 * pr + r % 2
                        w = par[:, col(l, L_CW, c * TAPS + t):col(l, L_CW, c * TAPS + t) + 1]
                        if t == 0:
                            dve.wait_ge(glu_done, 4 * l + pr + 1)
                            b = par[:, col(l, L_CB, c):col(l, L_CB, c) + 1]
                            nc.vector.tensor_scalar(work[:, c, :], conv_in[:, c, 0:T], w, b, ALU.mult,
                                                    ALU.add).then_inc(conv_step, 1)
                        else:
                            dve.wait_ge(conv_step, taps_total * l + s - 1)
                            nc.vector.scalar_tensor_tensor(out=work[:, c, :], in0=conv_in[:, c, t:t + T], scalar=w,
                                                           in1=work[:, c, :], op0=ALU.mult,
                                                           op1=ALU.add).then_inc(conv_step, 1)
                    return min(last, taps_total)

                done = 0
                for i in range(4):
                    lo(base + 2 * i + RING)
                    if i > 0:
                        done = conv(done, done + 10)
                    lo(base + 2 * i + 1 + RING)
                    dve.wait_ge(evac_done, 25 * l + 2 * i + 2)
                    nc.vector.tensor_tensor(conv_in[:, 2 * i:2 * i + 2, PAD:], tmp_a[:], tmp_b[:],
                                            ALU.mult).then_inc(glu_done, 1)
                    done = conv(done, done + 8)
                for i in range(M_QK, M_V):
                    lo(base + i + RING)
                    done = conv(done, done + 10)

                def rope_pair(g):
                    for w in range(2):
                        r = 6 * l + 2 * g + w
                        dve.wait_ge(rot_done, r + 1)
                        if r > 0:
                            dve.wait_ge(rope_done, r)
                        cos = rope_sb[:, 0:1, :].broadcast_to([P, 2, T])
                        sin = rope_sb[:, 1:2, :].broadcast_to([P, 2, T])
                        nc.vector.tensor_tensor(tmp_a[:], qk[:, g, w, :, :], cos, ALU.mult).then_inc(rope_mul, 1)
                        nc.vector.tensor_tensor(tmp_b[:], pair((2, 7)[w]), sin, ALU.mult).then_inc(rope_mul, 1)
                        dve.wait_ge(rope_mul, 2 * r + 2)
                        nc.vector.tensor_tensor(qk[:, g, w, :, :], tmp_a[:], tmp_b[:], ALU.add).then_inc(rope_done, 1)

                for g in range(NG):
                    lo(base + M_V + g + RING)
                    rope_pair(g)
                    done = conv(done, done + 6)

                def gate_panel(i):
                    lo(base + M_G + i + RING)

                def masked(h):
                    for q in range(TT):
                        u = 2 * h + q
                        n = 2 * HPG * l + u
                        keys = (q + 1) * P
                        dve.wait_ge(score_done, n + 1)
                        nc.vector.scalar_tensor_tensor(out=probs[q], in0=(S1 if q else S0), scalar=HD ** -0.5,
                                                       in1=mask_sb[:, q, :, 0:keys], op0=ALU.mult,
                                                       op1=ALU.add).then_inc(masked_done, 1)
                    for q in range(TT):
                        u = 2 * h + q
                        n = 2 * HPG * l + u
                        dve.wait_ge(masked_done, n + 1)
                        nc.vector.tensor_reduce(negmax[:, u:u + 1], probs[q], AX.XY, ALU.max,
                                                negate=True).then_inc(max_done, 1)

                def normalise(h):
                    for q in range(TT):
                        u = 2 * h + q
                        n = 2 * HPG * l + u
                        dve.wait_ge(exp_done, n + 1)
                        nc.vector.reciprocal(rden[:, u:u + 1], den[:, u:u + 1]).then_inc(rden_done, 1)
                        dve.wait_ge(rden_done, n + 1)
                        nc.vector.tensor_scalar(probs[q], probs[q], rden[:, u:u + 1], None,
                                                ALU.mult).then_inc(prob_done, 1)

                def head_out(c):
                    dve.wait_ge(o_hi_done, 2 * l + c + 1)
                    nc.vector.tensor_tensor(mid_lo[:, c, :], ps[:, 6 + c, 0:T], mid_hi[:, c, :].bitcast(F32),
                                            ALU.subtract).then_inc(o_lo_done, 1)

                for h in range(HPG):
                    if h == 0:
                        gate_panel(0)
                    masked(h)
                    done = conv(done, done + 4)
                    normalise(h)
                    if h < 3:
                        gate_panel(2 * h + 1)
                        done = conv(done, done + 8)
                        gate_panel(2 * h + 2)
                        if h == 2:
                            head_out(0)
                    done = conv(done, done + 6)
                head_out(1)
                conv(done, taps_total)

                dve.wait_ge(ln_sum, 2 * l + 1)
                for k in range(KC):
                    nc.vector.scalar_tensor_tensor(out=work[:, k, :], in0=ps[:, B_STAT, 0:T], scalar=-1.0 / D,
                                                   in1=work[:, k, :], op0=ALU.mult, op1=ALU.add).then_inc(xc_done, 1)
                dve.wait_ge(gates_done, 2 * l + 1)
                for i in range(4):
                    if i < 3:
                        dve.wait_ge(ao_done, 3 * l + i + 1)
                    else:
                        dve.wait_ge(panel_done, base + M_AO + 1)
                    nc.vector.tensor_tensor(y_attn[:, 2 * i:2 * i + 2, :], pair(i), gates[:, 2 * i:2 * i + 2, :],
                                            ALU.mult).then_inc(ya_done, 1)
                lo(base + M_AO + RING)
                recip(l, ln_std, ln_rstd)
                for k in range(KC + 2):
                    if k < KC:
                        dve.wait_ge(ln_sq, KC * (l + 1))
                        nc.vector.scalar_tensor_tensor(out=conv_in[:, k, PAD:], in0=work[:, k, :],
                                                       scalar=par[:, col(l, L_LG, k):col(l, L_LG, k) + 1], in1=rstd[:],
                                                       op0=ALU.mult, op1=ALU.mult).then_inc(ln_t, 1)
                    if k > 1:
                        dve.wait_ge(ln_hi, KC * l + k - 1)
                        split_lo(hA_lo[:, k - 2, :], work[:, k - 2, :], hA_hi[:, k - 2, :]).then_inc(ln_lo, 1)
                for i in range(4):
                    dve.wait_ge(panel_done, base + M_CO + i + 1)
                    dve.wait_ge(gates_done, 2 * l + 2)
                    nc.vector.tensor_tensor(tmp_a[:], pair(4 + i % 2), gates[:, 8 + 2 * i:10 + 2 * i, :],
                                            ALU.mult).then_inc(yc_done, 1)
                    dve.wait_ge(yc_done, 4 * l + i + 1)
                    if i > 0:
                        dve.wait_ge(y_lo_done, 4 * l + i)
                    nc.vector.tensor_tensor(tmp_b[:], tmp_a[:], y_attn[:, 2 * i:2 * i + 2, :], ALU.add).then_inc(y_done, 1)
                    dve.wait_ge(y_hi_done, 4 * l + i + 1)
                    split_lo(hB_lo[:, 2 * i:2 * i + 2, :], tmp_b[:], hB_hi[:, 2 * i:2 * i + 2, :]).then_inc(y_lo_done, 1)
                    lo(base + M_CO + i + RING)
                g = 3 * l + 1
                dve.wait_ge(gate_done, g + 1)
                for i in range(4):
                    dve.wait_ge(panel_done, base + M_WO + i + 1)
                    for o in (2 * i, 2 * i + 1):
                        nc.vector.scalar_tensor_tensor(out=x[:, o, :], in0=pair(i)[:, o % 2, :], scalar=gate[:, g, o:o + 1],
                                                       in1=x[:, o, :], op0=ALU.mult, op1=ALU.add).then_inc(x_done, 1)
                    if i < 3:
                        lo(base + M_WO + i + RING)

            def first_group(n0, a, b):
                for n in range(n0, n0 + KC):
                    dve.wait_ge(ada_in[n % 2], 16 * (n // 2 + 1))
                    if n:
                        dve.wait_ge(ada_step, n)
                    k = n % KC
                    nc.vector.scalar_tensor_tensor(out=ada_acc[0][:, a:b], in0=ada_raw[n % 2][:, a:b],
                                                   scalar=c_act[:, k:k + 1], in1=ada_acc[0][:, a:b],
                                                   op0=ALU.mult, op1=ALU.add).then_inc(ada_step, 1)

            nc.vector.memset(ones[:], 1.0).then_inc(setup_done, 1)
            nc.vector.memset(zeros[:], 0.0).then_inc(setup_done, 1)
            nc.vector.memset(eps[:], EPS).then_inc(setup_done, 1)
            nc.vector.memset(conv_in[:], 0.0).then_inc(setup_done, 1)
            nc.vector.memset(ada_acc[0], 0.0).then_inc(cleared, 1)
            dve.wait_ge(cleared, 1)
            dve.wait_ge(c_ready, 1)
            first_group(0, 0, 2 * D)
            add_bias(0, 0, 0, 2 * KC)
            finish_gain(0)
            lo(0)
            lo(1)
            for l in range(DEPTH):
                ffn(2 * l)
                mix(l)
                ffn(2 * l + 1)
            norm(3 * DEPTH)


def kernel(**inputs):
    import numpy as np
    import concourse.bacc as bacc
    from concourse.bass_utils import run_bass_kernel_spmd

    def columns(a):
        a = np.asarray(a)
        n = a.shape[-1] // P
        return a.reshape(-1, n, P).transpose(2, 0, 1).reshape(P, -1)

    a = {k: np.asarray(v) for k, v in inputs.items()}
    parts = [columns(a["c"]), columns(a["final_g"])]
    for l in range(DEPTH):
        taps = a["conv_w"][l].reshape(TAPS, KC, P).transpose(2, 1, 0).reshape(P, KC * TAPS)
        parts += [columns(a["ada_b"][l]), columns(a["norm_g"][l]), taps, columns(a["conv_b"][l]),
                  columns(a["conv_ln_g"][l]), columns(a["conv_ln_b"][l])]
    params = np.concatenate(parts, axis=1)
    xT = a["x"].reshape(T, KC, P).transpose(2, 1, 0)

    import ml_dtypes
    half = HD // 2
    inv_freq = (np.float32(10000.0) ** (-(np.arange(half, dtype=np.float32) * np.float32(2.0) / np.float32(HD)))).astype(np.float32)
    ang = np.arange(T, dtype=np.float32)[None, :] * inv_freq[:, None]
    rows = np.arange(P) % half
    rope = np.stack([np.cos(ang)[rows], np.sin(ang)[rows]], axis=1).astype(np.float32)
    perm = np.zeros((P, 2, P), np.float32)
    for r in range(P):
        if r % HD < half:
            perm[r + half, 0, r] = -1.0
        else:
            perm[r - half, 0, r] = 1.0
        perm[r, 1, r] = 1.0
    mask = np.zeros((P, TT, NG, T), np.float32)
    dist = (np.arange(T).reshape(TT, P).T)[:, :, None] - np.arange(T)[None, None, :]
    for g in range(NG):
        ok = (dist >= 0) & (dist <= WINDOW[g]) & (dist % DILATION[g] == 0)
        mask[:, :, g, :] = np.where(ok, 0.0, -1e30)
    arrays = {
        "xT": xT, "params": params, "rope": rope, "perm": perm, "mask": mask.astype(ml_dtypes.bfloat16),
        "ada_w": a["ada_w"], "ffn_wg": a["ffn_wg"], "ffn_wu": a["ffn_wu"], "ffn_wd": a["ffn_wd"], "w_in": a["w_in"],
        "attn_wo": a["attn_wo"], "conv_wo": a["conv_wo"], "w_out": a["w_out"],
    }
    nc = bacc.Bacc("TRN2", target_bir_lowering=False, num_devices=1)
    arrays = {f"in_{k}": np.ascontiguousarray(v) for k, v in arrays.items()}
    args = [nc.dram_tensor(k, v.shape, mybir.dt.from_np(v.dtype), kind="ExternalInput").ap() for k, v in arrays.items()]
    out = nc.dram_tensor("out_T", (P, KC, T), F32, kind="ExternalOutput").ap()
    decoder_program(nc, *args, out)
    r = run_bass_kernel_spmd(nc, [arrays], core_ids=[0])
    got = r.results[0]["out_T"]
    return got.transpose(2, 1, 0).reshape(1, T, D)
```

```python
from contextlib import ExitStack

import concourse.bass as bass
from concourse import mybir

ALU = mybir.AluOpType
ACT = mybir.ActivationFunctionType
AX = mybir.AxisListType
F32 = mybir.dt.float32
F32R = mybir.dt.float32r
BF16 = mybir.dt.bfloat16

P = 128
D = 1024
T = 256
DEPTH = 2
KC = D // P
TT = T // P
FF = 2816
FB = FF // 256
HD = 64
HPG = 4
NG = 3
DILATION = (1, 4, 16)
WINDOW = (128, 512, 2048)
TAPS = 31
PAD = TAPS - 1
GROUPS = 3 * DEPTH
GW = 3 * D
EPS = 1e-6
PW = KC * 256
RING = 3

FFN_PANELS = 3 * FB
M_U, M_QK, M_GA0, M_V, M_G, M_AO, M_CO, M_WO = 0, 8, 14, 15, 18, 25, 26, 30
MIX_PANELS = 34
LAYER_PANELS = 2 * FFN_PANELS + MIX_PANELS
PANELS = DEPTH * LAYER_PANELS

C_C = 0
C_FG = C_C + KC
C_LAYER = C_FG + KC
L_ADAB, L_NG, L_CW = 0, 9 * KC, 12 * KC
L_CB = L_CW + TAPS * KC
L_LG, L_LB = L_CB + KC, L_CB + 2 * KC
L_W = L_CB + 3 * KC
NPAR = C_LAYER + DEPTH * L_W


def col(layer, which, n=0):
    return C_LAYER + layer * L_W + which + n


def decoder_program(nc, xT, params, rope, perm, mask, ada_w, ffn_wg, ffn_wu, ffn_wd, w_in, attn_wo, conv_wo, w_out, out):
    with ExitStack() as ctx:
        def sb(name, shape, dt=F32):
            return ctx.enter_context(nc.sbuf_tensor(name, shape, dt))

        def sem(name):
            return ctx.enter_context(nc.semaphore(name))

        raw = sb("raw", [P, RING, PW])
        w_hi = sb("w_hi", [P, RING, PW], F32R)
        w_lo = sb("w_lo", [P, RING, PW], F32R)
        x = sb("x", [P, KC, T])
        work = sb("work", [P, KC, T])
        hA_hi = sb("hA_hi", [P, KC, T], F32R)
        hA_lo = sb("hA_lo", [P, KC, T], F32R)
        hB_hi = sb("hB_hi", [P, KC, T], F32R)
        hB_lo = sb("hB_lo", [P, KC, T], F32R)
        conv_in = sb("conv_in", [P, KC, PAD + T])
        v_sb = sb("v_sb", [P, TT, NG * 256])
        tmp_a = sb("tmp_a", [P, 2, T])
        tmp_b = sb("tmp_b", [P, 2, T])
        mid_hi = sb("mid_hi", [P, 2, T], F32R)
        mid_lo = sb("mid_lo", [P, 2, T], F32R)
        mask_sb = sb("mask_sb", [P, TT, NG, T], BF16)
        rope_sb = sb("rope_sb", [P, 2, T])
        perm_sb = sb("perm_sb", [P, 2, P])
        par = sb("par", [P, NPAR])
        ones = sb("ones", [P, P])
        zeros = sb("zeros", [P, 512], BF16)
        c_act = sb("c_act", [P, KC])
        mods = sb("mods", [P, GROUPS, 3 * KC])
        gs = sb("gs", [P, GROUPS, KC])
        gate = sb("gate", [P, GROUPS, KC])
        std = sb("std", [P, T])
        rstd = sb("rstd", [P, T])
        eps = sb("eps", [P, 1])
        spare = sb("spare", [P, 1])
        rowmax = sb("rowmax", [P, 2 * HPG])
        negmax = sb("negmax", [P, 2 * HPG])
        den = sb("den", [P, 2 * HPG])
        rden = sb("rden", [P, 2 * HPG])
        arena = sb("arena", [P, 4 * GW])
        ada_raw = [arena[:, i * GW:(i + 1) * GW] for i in range(2)]
        ada_acc = [arena[:, (2 + i) * GW:(3 + i) * GW] for i in range(2)]
        gates = arena[:, 0:16 * T].rearrange("p (c t) -> p c t", t=T)
        y_attn = arena[:, 16 * T:24 * T].rearrange("p (c t) -> p c t", t=T)
        first_raw = [arena[:, i * 2 * D:(i + 1) * 2 * D] for i in (0, 1, 2)] + [arena[:, 3 * GW:3 * GW + 2 * D]]
        o = 24 * T
        qk = arena[:, o:o + 12 * T].rearrange("p (g w c t) -> p g w c t", g=NG, w=2, t=T)
        o += 12 * T
        probs = [arena[:, o + 3 * T:o + 3 * T + 3 * P].rearrange("p (g t) -> p g t", g=NG),
                 arena[:, o:o + 3 * T].rearrange("p (g t) -> p g t", g=NG)]
        o += 3 * T + 3 * P
        probsT = arena[:, o:o + 6 * T].rearrange("p (g k t) -> p g k t", g=NG, k=TT)
        assert o + 6 * T <= 4 * GW

        ps = ctx.enter_context(nc.psum_tensor("ps", [P, 8, 512], F32))
        B_G, B_U, B_STAT, B_ADA = 4, 5, 6, 7
        KBANK = (3, 4, 5)
        S1 = ps[:, 0:2, :].rearrange("p b n -> p (b n)")[:, 0:NG * T].rearrange("p (g t) -> p g t", g=NG)
        S0 = ps[:, 2, 0:NG * P].rearrange("p (g t) -> p g t", g=NG)
        T1 = ps[:, 0:2, :].rearrange("p b n -> p (b n)")[:, 0:6 * P].rearrange("p (g k t) -> p g k t", g=NG, k=TT)
        T0 = S0

        def pair(bank):
            return ps[:, bank, :].rearrange("p (c t) -> p c t", t=T)

        def acc(o):
            return ps[:, o // 2, (o % 2) * T:(o % 2 + 1) * T]

        consts_in = sem("consts_in")
        tables_in = sem("tables_in")
        masks_in = sem("masks_in")
        x_in = sem("x_in")
        first_in = [sem(f"first_in{i}") for i in range(4)]
        raw_in = [sem(f"raw_in{i}") for i in range(RING)]
        ada_in = [sem(f"ada_in{i}") for i in range(2)]
        out_done = sem("out_done")
        setup_done = sem("setup_done")
        c_ready = sem("c_ready")
        hi_done, lo_done, panel_done = sem("hi_done"), sem("lo_done"), sem("panel_done")
        ada_step, mods_done, mods_step = sem("ada_step"), sem("mods_done"), sem("mods_step")
        ada_turned, ada_reduced = sem("ada_turned"), sem("ada_reduced")
        sq_done, ssq_done, std_done, rstd_done = sem("sq_done"), sem("ssq_done"), sem("std_done"), sem("rstd_done")
        t_done, h_hi_done, h_lo_done = sem("t_done"), sem("h_hi_done"), sem("h_lo_done")
        silu_done, mid_done, mid_hi_done, mid_lo_done = sem("silu_done"), sem("mid_done"), sem("mid_hi_done"), sem("mid_lo_done")
        acc_done, x_done = sem("acc_done"), sem("x_done")
        evac_done, glu_done, conv_step = sem("evac_done"), sem("glu_done"), sem("conv_step")
        rot_done, rope_mul, rope_done = sem("rot_done"), sem("rope_mul"), sem("rope_done")
        score_done, masked_done, max_done, exp_done = sem("score_done"), sem("masked_done"), sem("max_done"), sem("exp_done")
        rden_done, prob_done, turn_done, probT_done = sem("rden_done"), sem("prob_done"), sem("turn_done"), sem("probT_done")
        pv_done, o_hi_done, o_lo_done = sem("pv_done"), sem("o_hi_done"), sem("o_lo_done")
        gates_done = sem("gates_done")
        ln_sum, xc_done, ln_sq, ln_std, ln_rstd = sem("ln_sum"), sem("xc_done"), sem("ln_sq"), sem("ln_std"), sem("ln_rstd")
        ln_t, ln_silu, ln_hi, ln_lo = sem("ln_t"), sem("ln_silu"), sem("ln_hi"), sem("ln_lo")
        ao_done, ya_done, yc_done, y_done, y_hi_done, y_lo_done = (
            sem("ao_done"), sem("ya_done"), sem("yc_done"), sem("y_done"), sem("y_hi_done"), sem("y_lo_done"))
        final_done = sem("final_done")
        cleared = sem("cleared")
        gate_done = sem("gate_done")

        wg_v = ffn_wg.rearrange("l f (k p) n -> l f p k n", p=P)
        wu_v = ffn_wu.rearrange("l f (k p) n -> l f p k n", p=P)
        wd_v = ffn_wd.rearrange("l f (j k p) n -> l f j p k n", k=2, p=P)
        win_v = w_in.rearrange("l (k p) n -> l p k n", p=P)
        ao_v = attn_wo.rearrange("l (k p) n -> l p k n", p=P)
        co_v = conv_wo.rearrange("l (k p) n -> l p k n", p=P)
        wo_v = w_out.rearrange("l (k p) n -> l p k n", p=P)

        def kview(flat):
            return flat.rearrange("p (k n) -> p k n", k=KC)

        def dview(flat):
            return flat.rearrange("p (k n) -> p k n", k=2)

        QKV = NG * 256
        U0, GA0 = 3 * QKV, 3 * QKV + 2 * D
        win_cols = []
        for i in range(4):
            win_cols += [U0 + 256 * i, U0 + D + 256 * i]
        for g in range(NG):
            win_cols += [256 * g, QKV + 256 * g]
        win_cols += [GA0]
        win_cols += [2 * QKV + 256 * g for g in range(NG)]
        win_cols += [GA0 + 256 * i for i in range(1, 8)]

        def ffn_base(f):
            return (f // 2) * LAYER_PANELS + (f % 2) * (FFN_PANELS + MIX_PANELS)

        def mix_base(l):
            return l * LAYER_PANELS + FFN_PANELS

        def ada_before(f):
            return 2 * KC + (f // 2) * 3 * KC + (f % 2) * 2 * KC

        ADA_BANKS = (7, 6, 7, 6, 7, 6, 7, 4, 5, 7, 4, 5)

        def ada_batches(f):
            return 6 + (f // 2) * 18 + (f % 2) * 12

        def ada_groups(f):
            g = 3 * (f // 2) + (1 if f % 2 == 0 else 3)
            return [g, g + 1] if f % 2 == 0 else ([g] if g < GROUPS else [])

        def prod_end(f):
            return min(ffn_base(f) + FFN_PANELS + 2, PANELS)

        block = ctx.enter_context(nc.Block())

        @block.sync
        def _(sp):
            def load(p, dst_view, src):
                slot = p % RING
                if p >= RING:
                    sp.wait_ge(lo_done, p - RING + 1)
                sp.dma_start(dst_view(raw[:, slot, :]), src).then_inc(raw_in[slot], 16)

            sp.dma_start(par[:], params).then_inc(consts_in, 16)
            for k in range(KC):
                if k >= 4:
                    sp.wait_ge(ada_step, k - 3)
                sp.dma_start(first_raw[k % 4], ada_w[0, k * P:(k + 1) * P, 0:2 * D]).then_inc(first_in[k % 4], 16)
                if k == 2:
                    sp.dma_start(x[:], xT).then_inc(x_in, 16)
                    sp.dma_start(perm_sb[:], perm).then_inc(tables_in, 16)
            load(0, kview, wg_v[0, 0, :, :, 0:256])
            load(1, kview, wu_v[0, 0, :, :, 0:256])
            load(2, kview, wg_v[0, 0, :, :, 256:512])
            for k in range(4):
                sp.wait_ge(ada_step, 5 + k)
                sp.dma_start(first_raw[k].rearrange("p (r n) -> p r n", r=2),
                             ada_w[0, 2 * k * P:2 * (k + 1) * P, 2 * D:GW].rearrange("(r p) n -> p r n", p=P)
                             ).then_inc(first_in[k], 16)
            sp.dma_start(rope_sb[:], rope).then_inc(masks_in, 16)
            sp.dma_start(mask_sb[:], mask).then_inc(masks_in, 16)

            def ffn(f):
                l, s = f // 2, f % 2
                base = ffn_base(f)
                if f > 0:
                    load(base, kview, wg_v[l, s, :, :, 0:256])
                    load(base + 1, kview, wu_v[l, s, :, :, 0:256])
                else:
                    load(3, kview, wu_v[l, s, :, :, 256:512])
                    load(4, dview, wd_v[l, s, 0])
                with sp.Fori(0 if f else 1, FB - 1) as j:
                    p = base + 2
                    for i, (view, src) in enumerate((
                            (kview, wg_v[l, s, :, :, bass.ds(j * 256 + 256, 256)]),
                            (kview, wu_v[l, s, :, :, bass.ds(j * 256 + 256, 256)]),
                            (dview, wd_v[l, s, bass.ds(j, 1)].rearrange("o p k n -> (o p) k n")))):
                        slot = (p + i) % RING
                        sp.wait_ge(lo_done, j * 3 + (p + i - RING + 1))
                        sp.dma_start(view(raw[:, slot, :]), src).then_inc(raw_in[slot], 16)
                load(base + FFN_PANELS - 1, dview, wd_v[l, s, FB - 1])

            def mix(l):
                base = mix_base(l)
                for i, c in enumerate(win_cols):
                    load(base + i, kview, win_v[l, :, :, c:c + 256])
                load(base + M_AO, dview, ao_v[l])
                for i in range(4):
                    load(base + M_CO + i, kview, co_v[l, :, :, 256 * i:256 * i + 256])
                for i in range(4):
                    load(base + M_WO + i, kview, wo_v[l, :, :, 256 * i:256 * i + 256])

            for l in range(DEPTH):
                ffn(2 * l)
                mix(l)
                ffn(2 * l + 1)
            for k in range(KC):
                sp.wait_ge(final_done, k + 1)
                sp.dma_start(out[:, k, :], work[:, k, :]).then_inc(out_done, 16)
            sp.wait_ge(out_done, 16 * KC)

        @block.gpsimd
        def _(pool):
            nc.gpsimd.memset(ada_acc[0], 0.0).then_inc(cleared, 1)
            for f in range(2 * DEPTH):
                groups = ada_groups(f)
                if not groups:
                    continue
                pool.wait_ge(ada_step, ada_before(f))
                pool.wait_ge(mods_step, groups[0] + 1)
                if f % 2 == 1:
                    pool.wait_ge(x_done, KC * (3 * (f // 2) + 2))
                for i in range(len(groups)):
                    nc.gpsimd.memset(ada_acc[i], 0.0).then_inc(cleared, 1)
                with pool.Fori(0, KC) as j:
                    for i, g in enumerate(groups):
                        pool.wait_ge(ada_step, j * len(groups) + (ada_before(f) + (i - 1 if len(groups) == 2 else 0)))
                        src = ada_w[g // 3].rearrange("(k p) n -> k p n", p=P)[bass.ds(j, 1), :,
                                                                               (g % 3) * GW:(g % 3 + 1) * GW]
                        pool.dma_start(ada_raw[i], src.rearrange("o p n -> (o p) n")).then_inc(ada_in[i], 16)

        @block.tensor
        def _(pe):
            def three(out_ap, stat, mov, start, stop, **kw):
                nc.tensor.matmul(out_ap, stat[0], mov[0], start=start, stop=False, **kw)
                nc.tensor.matmul(out_ap, stat[0], mov[1], start=False, stop=False, **kw)
                return nc.tensor.matmul(out_ap, stat[1], mov[0], start=False, stop=stop, **kw)

            def k_panel(slot, rhs, bank, h_wait=None):
                hi, lo = kview(w_hi[:, slot, :]), kview(w_lo[:, slot, :])

                def tile(t, k, **kw):
                    c = slice(t * P, (t + 1) * P)
                    return three(pair(bank)[:, t, :], (hi[:, k, c], lo[:, k, c]), (rhs[0][:, k, :], rhs[1][:, k, :]),
                                 k == 0 and not (kw and t), k == KC - 1, **kw)

                if h_wait is None:
                    for t in range(2):
                        for k in range(KC):
                            mm = tile(t, k)
                else:
                    for k in range(KC):
                        h_wait(k)
                        for t in range(2):
                            mm = tile(t, k, skip_group_check=True)
                mm.then_inc(panel_done, 1)

            def split_ready(p):
                pe.wait_ge(hi_done, p + 1)
                pe.wait_ge(lo_done, p + 1)

            hA = (hA_hi, hA_lo)
            hB = (hB_hi, hB_lo)

            def column_sums(n_sem, done_sem, base, src):
                for k in range(KC):
                    pe.wait_ge(n_sem, base + k + 1)
                    mm = nc.tensor.matmul(ps[:, B_STAT, 0:T], ones[:], src(k), start=(k == 0), stop=(k == KC - 1))
                mm.then_inc(done_sem, 1)

            def square_sums(n, first, last):
                for k in range(first, last):
                    pe.wait_ge(sq_done, KC * n + k + 1)
                    mm = nc.tensor.matmul(ps[:, B_STAT, 0:T], ones[:], work[:, k, :], start=(k == 0), stop=(k == KC - 1))
                if last == KC:
                    mm.then_inc(ssq_done, 1)

            def ada_turn(m, bank, units, which, b):
                pe.wait_ge(ada_step, units)
                if m >= 2:
                    pe.wait_ge(ada_reduced, m - 1)
                for i in range(4):
                    c = 4 * b + i
                    mm = nc.tensor.transpose(ps[:, bank, i * P:(i + 1) * P], ada_acc[which][:, c * P:(c + 1) * P],
                                             perm_sb[:, 1, :])
                mm.then_inc(ada_turned, 1)

            def d_panel(slot, j_last=False, between=None):
                hi, lo = dview(w_hi[:, slot, :]), dview(w_lo[:, slot, :])
                if not j_last:
                    for kk in range(2):
                        for o in range(KC):
                            c = slice(o * P, (o + 1) * P)
                            mm = three(acc(o), (hi[:, kk, c], lo[:, kk, c]), (mid_hi[:, kk, :], mid_lo[:, kk, :]),
                                       False, False, skip_group_check=True)
                    mm.then_inc(panel_done, 1)
                else:
                    for o in range(KC):
                        for kk in range(2):
                            c = slice(o * P, (o + 1) * P)
                            mm = three(acc(o), (hi[:, kk, c], lo[:, kk, c]), (mid_hi[:, kk, :], mid_lo[:, kk, :]),
                                       False, kk == 1, skip_group_check=True)
                        if o % 2 == 1:
                            mm.then_inc(acc_done if o < KC - 1 else panel_done, 1)
                            between(o // 2)

            def ffn(f):
                base = ffn_base(f)
                n = 3 * (f // 2) + 2 * (f % 2)
                if f > 0:
                    pe.wait_ge(x_done, KC * n)
                for b in range(4):
                    nc.tensor.matmul(ps[:, b, :], zeros[:, 0:P], zeros[:, :], start=True, stop=False,
                                     skip_group_check=True)
                split_ready(base)
                k_panel(base % RING, hA, B_G, lambda k: pe.wait_ge(h_lo_done, KC * n + k + 1))
                split_ready(base + 1)
                k_panel((base + 1) % RING, hA, B_U)
                if f == 0:
                    for b in (4, 5):
                        ada_turn(b, (B_ADA, B_STAT)[b % 2], 2 * KC, 0, b)
                with pe.Fori(0, FB - 2) as j:
                    p = base + 2
                    pe.wait_ge(hi_done, j * 3 + (p + 1))
                    pe.wait_ge(lo_done, j * 3 + (p + 1))
                    pe.wait_ge(silu_done, j + (f * FB + 1))
                    k_panel(p % RING, hA, B_G)
                    pe.wait_ge(hi_done, j * 3 + (p + 2))
                    pe.wait_ge(lo_done, j * 3 + (p + 2))
                    pe.wait_ge(mid_done, j + (f * FB + 1))
                    k_panel((p + 1) % RING, hA, B_U)
                    pe.wait_ge(hi_done, j * 3 + (p + 3))
                    pe.wait_ge(lo_done, j * 3 + (p + 3))
                    pe.wait_ge(mid_lo_done, j + (f * FB + 1))
                    d_panel((p + 2) % RING)
                nb = 6 * len(ada_groups(f))

                def turns(*which):
                    for i in which:
                        if i < nb:
                            ada_turn(ada_batches(f) + i, ADA_BANKS[i], ada_before(f) + KC * len(ada_groups(f)),
                                     i // 6, i % 6)

                p = base + 2 + 3 * (FB - 2)
                turns(0, 1)
                split_ready(p)
                pe.wait_ge(silu_done, f * FB + FB - 1)
                k_panel(p % RING, hA, B_G)
                turns(2, 3)
                split_ready(p + 1)
                pe.wait_ge(mid_done, f * FB + FB - 1)
                k_panel((p + 1) % RING, hA, B_U)
                turns(4, 5)
                split_ready(p + 2)
                pe.wait_ge(mid_lo_done, f * FB + FB - 1)
                d_panel((p + 2) % RING)
                split_ready(p + 3)
                pe.wait_ge(mid_lo_done, f * FB + FB)
                turns(6, 7)

                def between(i):
                    if i == 0:
                        turns(8, 9)
                    elif i == 1:
                        turns(10, 11)
                    elif i == 2:
                        square_sums(n + 1, 0, 2)
                    else:
                        square_sums(n + 1, 2, KC)

                d_panel((p + 3) % RING, True, between)

            def mix(l):
                base = mix_base(l)
                e0 = 25 * l
                first = base

                n = 3 * l + 1
                for i in range(RING):
                    split_ready(first + i)
                    k_panel((first + i) % RING, hA, KBANK[(first + i) % RING],
                            (lambda k: pe.wait_ge(h_lo_done, KC * n + k + 1)) if i == 0 else None)
                with pe.Fori(0, 4) as j:
                    for i in range(RING):
                        q = first + RING + i
                        pe.wait_ge(hi_done, j * RING + (q + 1))
                        pe.wait_ge(lo_done, j * RING + (q + 1))
                        pe.wait_ge(evac_done, j * RING + (e0 + i + 1))
                        k_panel(q % RING, hA, KBANK[q % RING])

                def v_panel(g):
                    p = base + M_V + g
                    slot = p % RING
                    split_ready(p)
                    pe.wait_ge(evac_done, e0 + M_V + g - RING + 1)
                    hi, lo = kview(w_hi[:, slot, :]), kview(w_lo[:, slot, :])
                    for t in range(TT):
                        c = slice(t * P, (t + 1) * P)
                        for k in range(KC):
                            mm = three(pair(KBANK[slot])[:, t, :], (hA_hi[:, k, c], hA_lo[:, k, c]),
                                       (hi[:, k, :], lo[:, k, :]), k == 0, k == KC - 1)
                    mm.then_inc(panel_done, 1)

                pe.wait_ge(masks_in, 32)

                def rotate(g):
                    for w in range(2):
                        r = 6 * l + 2 * g + w
                        pe.wait_ge(evac_done, e0 + M_QK + 2 * g + w + 1)
                        if r % 6 >= 2:
                            pe.wait_ge(rope_done, r - 1)
                        for c in range(2):
                            mm = nc.tensor.matmul(pair((2, 7)[w])[:, c, :], perm_sb[:, 0, :], qk[:, g, w, c, :],
                                                  start=True, stop=True)
                        mm.then_inc(rot_done, 1)

                for g in range(NG):
                    v_panel(g)
                    rotate(g)

                def gate_panel(i):
                    p = base + M_G + i
                    split_ready(p)
                    pe.wait_ge(evac_done, e0 + M_G + i - RING + 1)
                    k_panel(p % RING, hA, KBANK[p % RING])

                def scores(h):
                    if h == 0:
                        pe.wait_ge(rope_done, 6 * (l + 1))
                    else:
                        pe.wait_ge(probT_done, 2 * (HPG * l + h))
                    for q in range(TT):
                        keys = (q + 1) * P
                        for g in range(NG):
                            head = HPG * g + h
                            part = slice((head % 2) * HD, (head % 2 + 1) * HD)
                            c = (head // 2) % 2
                            dst = S1[:, g, :] if q else S0[:, g, :]
                            mm = nc.tensor.matmul(dst, qk[part, g, 0, c, q * P:(q + 1) * P], qk[part, g, 1, c, 0:keys],
                                                  start=True, stop=True)
                        mm.then_inc(score_done, 1)

                def turn(h):
                    for q in range(TT):
                        pe.wait_ge(prob_done, 2 * (HPG * l + h) + q + 1)
                        for g in range(NG):
                            for k in range(q + 1):
                                dst = T1[:, g, k, :] if q else T0[:, g, :]
                                mm = nc.tensor.transpose(dst, probs[q][:, g, k * P:(k + 1) * P], perm_sb[:, 1, :])
                        mm.then_inc(turn_done, 1)

                def pv(h):
                    pe.wait_ge(probT_done, 2 * (HPG * l + h + 1))
                    half = slice((h % 2) * HD, (h % 2 + 1) * HD)
                    bank = 6 + h // 2
                    for g in range(NG):
                        cols = slice((HPG * g + h) * HD, (HPG * g + h + 1) * HD)
                        nc.tensor.matmul(ps[half, bank, 0:T], v_sb[:, 0, cols], probsT[:, g, 0, :],
                                         start=(g == 0), stop=False)
                        mm = nc.tensor.matmul(ps[half, bank, P:T], v_sb[:, 1, cols], probsT[:, g, 1, P:T],
                                              start=False, stop=(g == NG - 1))
                    mm.then_inc(pv_done, 1)

                gate_panel(0)
                scores(0)
                gate_panel(1)
                turn(0)
                gate_panel(2)
                pv(0)
                scores(1)
                gate_panel(3)
                turn(1)
                gate_panel(4)
                pv(1)
                scores(2)
                gate_panel(5)
                turn(2)
                gate_panel(6)
                pv(2)
                scores(3)
                turn(3)
                pv(3)

                p = base + M_AO
                split_ready(p)
                pe.wait_ge(o_lo_done, 2 * (l + 1))
                hi, lo = dview(w_hi[:, p % RING, :]), dview(w_lo[:, p % RING, :])
                for i in range(4):
                    if i == 3:
                        pe.wait_ge(evac_done, e0 + 25)
                    for t in range(2):
                        c = slice((2 * i + t) * P, (2 * i + t + 1) * P)
                        for kk in range(2):
                            mm = three(pair(i)[:, t, :], (hi[:, kk, c], lo[:, kk, c]), (mid_hi[:, kk, :], mid_lo[:, kk, :]),
                                       kk == 0, kk == 1)
                    mm.then_inc(ao_done if i < 3 else panel_done, 1)

                pe.wait_ge(conv_step, KC * TAPS * (l + 1))
                for k in range(KC):
                    mm = nc.tensor.matmul(ps[:, B_STAT, 0:T], ones[:], work[:, k, :], start=(k == 0), stop=(k == KC - 1))
                mm.then_inc(ln_sum, 1)
                pe.wait_ge(xc_done, KC * (l + 1))
                column_sums(ln_sq, ln_sum, KC * l, lambda k: conv_in[:, k, PAD:])

                for i in range(4):
                    p = base + M_CO + i
                    split_ready(p)
                    pe.wait_ge(ya_done, 4 * (l + 1))
                    if i >= 2:
                        pe.wait_ge(yc_done, 4 * l + i - 1)
                    if i == 0:
                        k_panel(p % RING, hA, 4 + i % 2, lambda k: pe.wait_ge(ln_lo, KC * l + k + 1))
                    else:
                        k_panel(p % RING, hA, 4 + i % 2)
                for i in range(4):
                    p = base + M_WO + i
                    split_ready(p)
                    k_panel(p % RING, hB, i, (lambda k: pe.wait_ge(y_lo_done, 4 * l + k // 2 + 1)) if i == 0 else None)
                    if i >= 2:
                        square_sums(3 * l + 2, 2 * (i - 2), 2 * (i - 1))
                square_sums(3 * l + 2, 4, KC)

            pe.wait_ge(setup_done, 4)
            pe.wait_ge(tables_in, 16)
            square_sums(0, 0, KC)
            for b in range(4):
                ada_turn(b, (B_ADA, B_U)[b % 2], KC, 0, b)
            for l in range(DEPTH):
                ffn(2 * l)
                mix(l)
                ffn(2 * l + 1)

        @block.scalar
        def _(act):
            def hi(p):
                slot = p % RING
                act.wait_ge(raw_in[slot], 16 * (p // RING + 1))
                if p >= RING:
                    act.wait_ge(panel_done, p - RING + 1)
                nc.scalar.copy(w_hi[:, slot, :], raw[:, slot, :]).then_inc(hi_done, 1)

            def hi_loop(j, p):
                slot = p % RING
                act.wait_ge(raw_in[slot], j * 16 + 16 * (p // RING + 1))
                act.wait_ge(panel_done, j * 3 + (p - RING + 1))
                nc.scalar.copy(w_hi[:, slot, :], raw[:, slot, :]).then_inc(hi_done, 1)

            def preload(func):
                nc.scalar.activation(spare[:], eps[:], func)

            def norm(n):
                preload(ACT.Sqrt)
                for k in range(KC):
                    if n > 0:
                        act.wait_ge(x_done, KC * (n - 1) + k + 1)
                    if n == 0 and k == 0:
                        act.wait_ge(x_in, 16)
                    nc.scalar.activation(work[:, k, :], x[:, k, :], ACT.Square).then_inc(sq_done, 1)
                act.wait_ge(ssq_done, n + 1)
                nc.scalar.activation(std[:], ps[:, B_STAT, 0:T], ACT.Sqrt, bias=eps[:, 0:1],
                                     scale=1.0 / D).then_inc(std_done, 1)
                if n == 3 * DEPTH:
                    return
                preload(ACT.Sigmoid if n % 3 == 1 else ACT.Silu)
                if n == 0:
                    hi(0)
                for k in range(KC):
                    act.wait_ge(t_done, KC * n + k + 1)
                    nc.scalar.activation(hA_hi[:, k, :], work[:, k, :], ACT.Identity,
                                         bias=mods[:, n, k:k + 1]).then_inc(h_hi_done, 1)

            def silu(f, j):
                nc.scalar.activation(tmp_a[:], pair(B_G), ACT.Silu).then_inc(silu_done, 1)

            def ffn(f):
                base = ffn_base(f)
                norm(3 * (f // 2) + 2 * (f % 2))
                if f == 0:
                    hi(1)
                hi(base + 2)
                act.wait_ge(panel_done, base + 1)
                silu(f, 0)
                hi(base + 3)
                hi(base + 4)
                act.wait_ge(mid_done, f * FB + 1)
                nc.scalar.copy(mid_hi[:], tmp_b[:]).then_inc(mid_hi_done, 1)
                last = ffn_base(f) + FFN_PANELS == PANELS
                n = FB - 2 if last else FB - 1
                with act.Fori(0, n) as j:
                    p = base + 2
                    act.wait_ge(panel_done, j * 3 + (p + 1))
                    act.wait_ge(mid_done, j + (f * FB + 1))
                    silu(f, j)
                    hi_loop(j, p + 3)
                    hi_loop(j, p + 4)
                    hi_loop(j, p + 5)
                    act.wait_ge(mid_done, j + (f * FB + 2))
                    nc.scalar.copy(mid_hi[:], tmp_b[:]).then_inc(mid_hi_done, 1)
                if last:
                    p = base + 2 + 3 * n
                    act.wait_ge(panel_done, p + 1)
                    silu(f, n)
                    hi(p + 3)
                    act.wait_ge(panel_done, p + 3)
                    act.wait_ge(mid_done, f * FB + FB)
                    nc.scalar.copy(mid_hi[:], tmp_b[:]).then_inc(mid_hi_done, 1)

            def mix(l):
                base = mix_base(l)
                norm(3 * l + 1)
                hi(base + 2)

                def panel(i, dst, func, src_t=None):
                    act.wait_ge(panel_done, base + i + 1)
                    nc.scalar.activation(dst, pair(KBANK[(base + i) % RING]), func).then_inc(evac_done, 1)
                    hi(base + i + RING)

                for i in range(4):
                    if i:
                        act.wait_ge(glu_done, 4 * l + i)
                    panel(2 * i, tmp_a[:], ACT.Copy)
                    panel(2 * i + 1, tmp_b[:], ACT.Sigmoid)
                for g in range(NG):
                    panel(M_QK + 2 * g, qk[:, g, 0, :, :], ACT.Copy)
                    panel(M_QK + 2 * g + 1, qk[:, g, 1, :, :], ACT.Copy)
                panel(M_GA0, gates[:, 0:2, :], ACT.Copy)
                for g in range(NG):
                    panel(M_V + g, v_sb[:, :, g * 256:(g + 1) * 256], ACT.Copy)

                def gate_panel(i):
                    panel(M_G + i, gates[:, 2 * (i + 1):2 * (i + 2), :], ACT.Copy)

                def exps(h):
                    for q in range(TT):
                        u = 2 * h + q
                        act.wait_ge(max_done, 2 * HPG * l + u + 1)
                        nc.scalar.activation(probs[q], probs[q], ACT.Exp, bias=negmax[:, u:u + 1],
                                             accum_out=den[:, u:u + 1]).then_inc(exp_done, 1)

                def turned(h):
                    if h > 0:
                        act.wait_ge(pv_done, HPG * l + h)
                    act.wait_ge(turn_done, 2 * (HPG * l + h) + 1)
                    nc.scalar.copy(probsT[:, :, 0, 0:P], T0).then_inc(probT_done, 1)
                    act.wait_ge(turn_done, 2 * (HPG * l + h) + 2)
                    nc.scalar.copy(probsT[:, :, :, P:T], T1).then_inc(probT_done, 1)

                def head_out(c):
                    act.wait_ge(pv_done, HPG * l + 2 * c + 2)
                    nc.scalar.copy(mid_hi[:, c, :], ps[:, 6 + c, 0:T]).then_inc(o_hi_done, 1)

                gate_panel(0)
                exps(0)
                gate_panel(1)
                turned(0)
                gate_panel(2)
                exps(1)
                gate_panel(3)
                turned(1)
                gate_panel(4)
                exps(2)
                head_out(0)
                gate_panel(5)
                turned(2)
                gate_panel(6)
                exps(3)
                turned(3)
                head_out(1)
                act.wait_ge(evac_done, 25 * (l + 1))
                nc.scalar.activation(gates[:, 0:8, :], gates[:, 0:8, :], ACT.Sigmoid).then_inc(gates_done, 1)
                nc.scalar.activation(gates[:, 8:16, :], gates[:, 8:16, :], ACT.Sigmoid).then_inc(gates_done, 1)
                hi(base + M_AO + 3)
                preload(ACT.Sqrt)
                for k in range(KC):
                    act.wait_ge(xc_done, KC * l + k + 1)
                    nc.scalar.activation(conv_in[:, k, PAD:], work[:, k, :], ACT.Square).then_inc(ln_sq, 1)
                act.wait_ge(ln_sum, 2 * (l + 1))
                nc.scalar.activation(std[:], ps[:, B_STAT, 0:T], ACT.Sqrt, bias=eps[:, 0:1],
                                     scale=1.0 / D).then_inc(ln_std, 1)
                preload(ACT.Silu)
                for k in range(KC):
                    act.wait_ge(ln_t, KC * l + k + 1)
                    nc.scalar.activation(work[:, k, :], conv_in[:, k, PAD:], ACT.Silu,
                                         bias=par[:, col(l, L_LB, k):col(l, L_LB, k) + 1]).then_inc(ln_silu, 1)
                    act.wait_ge(ln_silu, KC * l + k + 1)
                    nc.scalar.copy(hA_hi[:, k, :], work[:, k, :]).then_inc(ln_hi, 1)
                for i in range(4):
                    hi(base + M_CO + i + RING)
                    act.wait_ge(y_done, 4 * l + i + 1)
                    nc.scalar.copy(hB_hi[:, 2 * i:2 * i + 2, :], tmp_b[:]).then_inc(y_hi_done, 1)
                for i in range(3):
                    hi(base + M_WO + i + RING)

            act.wait_ge(consts_in, 16)
            act.wait_ge(setup_done, 4)
            nc.scalar.activation(c_act[:], par[:, C_C:C_C + KC], ACT.Silu).then_inc(c_ready, 1)
            for l in range(DEPTH):
                ffn(2 * l)
                mix(l)
                ffn(2 * l + 1)
            norm(3 * DEPTH)

        @block.vector
        def _(dve):
            def split_lo(dst, whole, hi_part):
                return nc.vector.tensor_tensor(dst, whole, hi_part.bitcast(F32), ALU.subtract)

            def lo(p):
                slot = p % RING
                dve.wait_ge(hi_done, p + 1)
                split_lo(w_lo[:, slot, :], raw[:, slot, :], w_hi[:, slot, :]).then_inc(lo_done, 1)

            def lo_loop(j, p):
                slot = p % RING
                dve.wait_ge(hi_done, j * 3 + (p + 1))
                split_lo(w_lo[:, slot, :], raw[:, slot, :], w_hi[:, slot, :]).then_inc(lo_done, 1)

            def recip(n, wait, done):
                dve.wait_ge(wait, n + 1)
                nc.vector.reciprocal(rstd[:], std[:]).then_inc(done, 1)
                dve.wait_ge(done, n + 1)

            def norm(n):
                recip(n, std_done, rstd_done)
                if n == 3 * DEPTH:
                    for k in range(KC):
                        nc.vector.scalar_tensor_tensor(out=work[:, k, :], in0=x[:, k, :],
                                                       scalar=par[:, C_FG + k:C_FG + k + 1], in1=rstd[:],
                                                       op0=ALU.mult, op1=ALU.mult).then_inc(final_done, 1)
                    return
                dve.wait_ge(mods_done, n + 1)
                for k in range(KC + 1):
                    if k < KC:
                        nc.vector.scalar_tensor_tensor(out=work[:, k, :], in0=x[:, k, :], scalar=gs[:, n, k:k + 1],
                                                       in1=rstd[:], op0=ALU.mult, op1=ALU.mult).then_inc(t_done, 1)
                    if k > 0:
                        dve.wait_ge(h_hi_done, KC * n + k)
                        dve.wait_ge(t_done, KC * n + k)
                        nc.vector.scalar_tensor_tensor(out=hA_lo[:, k - 1, :], in0=work[:, k - 1, :],
                                                       scalar=mods[:, n, k - 1:k], in1=hA_hi[:, k - 1, :].bitcast(F32),
                                                       op0=ALU.add, op1=ALU.subtract).then_inc(h_lo_done, 1)

            def reduce_turned(m, bank, g, b):
                dve.wait_ge(ada_turned, m + 1)
                nc.vector.tensor_reduce(mods[:, g, 4 * b:4 * b + 4], ps[:, bank, :].rearrange("p (c t) -> p c t", c=4),
                                        AX.X, ALU.add).then_inc(ada_reduced, 1)

            def add_bias(n, batches, g, first, last):
                dve.wait_ge(ada_reduced, batches)
                b = col(g // 3, L_ADAB, (g % 3) * 3 * KC)
                nc.vector.tensor_tensor(mods[:, g, first:last], mods[:, g, first:last], par[:, b + first:b + last],
                                        ALU.add).then_inc(mods_step, 1)
                dve.wait_ge(mods_step, n + 1)

            def finish_gate(g):
                nc.vector.tensor_scalar(gate[:, g, :], mods[:, g, 2 * KC:3 * KC], 1.0 if g % 3 == 1 else 0.5, None,
                                        ALU.mult).then_inc(gate_done, 1)

            def finish_gain(g):
                b = col(g // 3, L_NG, (g % 3) * KC)
                nc.vector.scalar_tensor_tensor(out=gs[:, g, :], in0=mods[:, g, KC:2 * KC], scalar=1.0,
                                               in1=par[:, b:b + KC], op0=ALU.add, op1=ALU.mult).then_inc(mods_done, 1)

            def hidden(f):
                nc.vector.tensor_tensor(tmp_b[:], tmp_a[:], pair(B_U), ALU.mult).then_inc(mid_done, 1)

            def ffn(f):
                base = ffn_base(f)
                n = 3 * (f // 2) + 2 * (f % 2)
                norm(n)
                if f == 0:
                    lo(1)
                lo(base + 2)
                if f == 0:
                    first_gate()
                lo(base + 3)
                dve.wait_ge(silu_done, f * FB + 1)
                dve.wait_ge(panel_done, base + 2)
                hidden(f)
                lo(base + 4)
                dve.wait_ge(mid_hi_done, f * FB + 1)
                split_lo(mid_lo[:], tmp_b[:], mid_hi[:]).then_inc(mid_lo_done, 1)
                groups = ada_groups(f)
                a0 = ada_before(f)
                if f == 0:
                    for b in (4, 5):
                        reduce_turned(b, (B_ADA, B_STAT)[b % 2], 0, b)
                    add_bias(1, 6, 0, 2 * KC, 3 * KC)
                    finish_gate(0)
                if groups:
                    dve.wait_ge(cleared, groups[-1] + 1)

                def body(j, units):
                    p = base + 2
                    lo_loop(j, p + 3)
                    dve.wait_ge(silu_done, j + (f * FB + 2))
                    dve.wait_ge(panel_done, j * 3 + (p + 2))
                    dve.wait_ge(mid_lo_done, j + (f * FB + 1))
                    hidden(f)
                    lo_loop(j, p + 4)
                    lo_loop(j, p + 5)
                    dve.wait_ge(mid_hi_done, j + (f * FB + 2))
                    split_lo(mid_lo[:], tmp_b[:], mid_hi[:]).then_inc(mid_lo_done, 1)
                    for i in range(units):
                        dve.wait_ge(ada_in[i], j * 16 + ada_dmas(f, i))
                        dve.wait_ge(ada_step, j * units + (a0 + (i - 1 if units == 2 else 0)))
                        nc.vector.scalar_tensor_tensor(out=ada_acc[i], in0=ada_raw[i], scalar=c_act[:, bass.ds(j, 1)],
                                                       in1=ada_acc[i], op0=ALU.mult, op1=ALU.add).then_inc(ada_step, 1)

                last = ffn_base(f) + FFN_PANELS == PANELS
                e = FB - 2
                with dve.Fori(0, KC) as j:
                    body(j, len(groups))
                with dve.Fori(KC, e) as j:
                    body(j, 0)

                def reduces(*which):
                    for i in which:
                        if i < 6 * len(groups):
                            reduce_turned(ada_batches(f) + i, ADA_BANKS[i], groups[i // 6], i % 6)
                            if i % 6 == 5:
                                g = groups[i // 6]
                                add_bias(g + 1, ada_batches(f) + i + 1, g, 0, 3 * KC)
                                finish_gain(g)
                                finish_gate(g)

                p = base + 2 + 3 * e
                reduces(0, 1)
                lo(p + 3)
                reduces(2, 3)
                dve.wait_ge(silu_done, f * FB + FB)
                dve.wait_ge(panel_done, p + 2)
                dve.wait_ge(mid_lo_done, f * FB + FB - 1)
                hidden(f)
                reduces(4, 5)
                if not last:
                    lo(p + 4)
                dve.wait_ge(mid_hi_done, f * FB + FB)
                split_lo(mid_lo[:], tmp_b[:], mid_hi[:]).then_inc(mid_lo_done, 1)
                if not last:
                    lo(p + 5)
                reduces(6, 7, 8, 9, 10, 11)
                dve.wait_ge(gate_done, n + 1)
                for i in range(4):
                    if i < 3:
                        dve.wait_ge(acc_done, 3 * f + i + 1)
                    else:
                        dve.wait_ge(panel_done, base + FFN_PANELS)
                    for o in (2 * i, 2 * i + 1):
                        nc.vector.scalar_tensor_tensor(out=x[:, o, :], in0=acc(o), scalar=gate[:, n, o:o + 1],
                                                       in1=x[:, o, :], op0=ALU.mult, op1=ALU.add).then_inc(x_done, 1)

            def ada_dmas(f, slot):
                n = 0
                for e in range(f):
                    n += KC if slot < len(ada_groups(e)) else 0
                return 16 * (n + 1)

            def mix(l):
                base = mix_base(l)
                norm(3 * l + 1)
                lo(base + 2)
                taps_total = KC * TAPS

                def conv(first, last):
                    for s in range(first, min(last, taps_total)):
                        pr, r = divmod(s, 2 * TAPS)
                        t, c = r // 2, 2 * pr + r % 2
                        w = par[:, col(l, L_CW, c * TAPS + t):col(l, L_CW, c * TAPS + t) + 1]
                        if t == 0:
                            dve.wait_ge(glu_done, 4 * l + pr + 1)
                            b = par[:, col(l, L_CB, c):col(l, L_CB, c) + 1]
                            nc.vector.tensor_scalar(work[:, c, :], conv_in[:, c, 0:T], w, b, ALU.mult,
                                                    ALU.add).then_inc(conv_step, 1)
                        else:
                            dve.wait_ge(conv_step, taps_total * l + s - 1)
                            nc.vector.scalar_tensor_tensor(out=work[:, c, :], in0=conv_in[:, c, t:t + T], scalar=w,
                                                           in1=work[:, c, :], op0=ALU.mult,
                                                           op1=ALU.add).then_inc(conv_step, 1)
                    return min(last, taps_total)

                done = 0
                for i in range(4):
                    lo(base + 2 * i + RING)
                    if i > 0:
                        done = conv(done, done + 10)
                    lo(base + 2 * i + 1 + RING)
                    dve.wait_ge(evac_done, 25 * l + 2 * i + 2)
                    nc.vector.tensor_tensor(conv_in[:, 2 * i:2 * i + 2, PAD:], tmp_a[:], tmp_b[:],
                                            ALU.mult).then_inc(glu_done, 1)
                    done = conv(done, done + 8)
                for i in range(M_QK, M_V):
                    lo(base + i + RING)
                    done = conv(done, done + 10)

                def rope_pair(g):
                    for w in range(2):
                        r = 6 * l + 2 * g + w
                        dve.wait_ge(rot_done, r + 1)
                        if r > 0:
                            dve.wait_ge(rope_done, r)
                        cos = rope_sb[:, 0:1, :].broadcast_to([P, 2, T])
                        sin = rope_sb[:, 1:2, :].broadcast_to([P, 2, T])
                        nc.vector.tensor_tensor(tmp_a[:], qk[:, g, w, :, :], cos, ALU.mult).then_inc(rope_mul, 1)
                        nc.vector.tensor_tensor(tmp_b[:], pair((2, 7)[w]), sin, ALU.mult).then_inc(rope_mul, 1)
                        dve.wait_ge(rope_mul, 2 * r + 2)
                        nc.vector.tensor_tensor(qk[:, g, w, :, :], tmp_a[:], tmp_b[:], ALU.add).then_inc(rope_done, 1)

                for g in range(NG):
                    lo(base + M_V + g + RING)
                    rope_pair(g)
                    done = conv(done, done + 6)

                def gate_panel(i):
                    lo(base + M_G + i + RING)

                def masked(h):
                    for q in range(TT):
                        u = 2 * h + q
                        n = 2 * HPG * l + u
                        keys = (q + 1) * P
                        dve.wait_ge(score_done, n + 1)
                        nc.vector.scalar_tensor_tensor(out=probs[q], in0=(S1 if q else S0), scalar=HD ** -0.5,
                                                       in1=mask_sb[:, q, :, 0:keys], op0=ALU.mult,
                                                       op1=ALU.add).then_inc(masked_done, 1)
                    for q in range(TT):
                        u = 2 * h + q
                        n = 2 * HPG * l + u
                        dve.wait_ge(masked_done, n + 1)
                        nc.vector.tensor_reduce(negmax[:, u:u + 1], probs[q], AX.XY, ALU.max,
                                                negate=True).then_inc(max_done, 1)

                def normalise(h):
                    for q in range(TT):
                        u = 2 * h + q
                        n = 2 * HPG * l + u
                        dve.wait_ge(exp_done, n + 1)
                        nc.vector.reciprocal(rden[:, u:u + 1], den[:, u:u + 1]).then_inc(rden_done, 1)
                        dve.wait_ge(rden_done, n + 1)
                        nc.vector.tensor_scalar(probs[q], probs[q], rden[:, u:u + 1], None,
                                                ALU.mult).then_inc(prob_done, 1)

                def head_out(c):
                    dve.wait_ge(o_hi_done, 2 * l + c + 1)
                    nc.vector.tensor_tensor(mid_lo[:, c, :], ps[:, 6 + c, 0:T], mid_hi[:, c, :].bitcast(F32),
                                            ALU.subtract).then_inc(o_lo_done, 1)

                for h in range(HPG):
                    if h == 0:
                        gate_panel(0)
                    masked(h)
                    done = conv(done, done + 4)
                    normalise(h)
                    if h < 3:
                        gate_panel(2 * h + 1)
                        done = conv(done, done + 8)
                        gate_panel(2 * h + 2)
                        if h == 2:
                            head_out(0)
                    done = conv(done, done + 6)
                head_out(1)
                conv(done, taps_total)

                dve.wait_ge(ln_sum, 2 * l + 1)
                for k in range(KC):
                    nc.vector.scalar_tensor_tensor(out=work[:, k, :], in0=ps[:, B_STAT, 0:T], scalar=-1.0 / D,
                                                   in1=work[:, k, :], op0=ALU.mult, op1=ALU.add).then_inc(xc_done, 1)
                dve.wait_ge(gates_done, 2 * l + 1)
                for i in range(4):
                    if i < 3:
                        dve.wait_ge(ao_done, 3 * l + i + 1)
                    else:
                        dve.wait_ge(panel_done, base + M_AO + 1)
                    nc.vector.tensor_tensor(y_attn[:, 2 * i:2 * i + 2, :], pair(i), gates[:, 2 * i:2 * i + 2, :],
                                            ALU.mult).then_inc(ya_done, 1)
                lo(base + M_AO + RING)
                recip(l, ln_std, ln_rstd)
                for k in range(KC + 2):
                    if k < KC:
                        dve.wait_ge(ln_sq, KC * (l + 1))
                        nc.vector.scalar_tensor_tensor(out=conv_in[:, k, PAD:], in0=work[:, k, :],
                                                       scalar=par[:, col(l, L_LG, k):col(l, L_LG, k) + 1], in1=rstd[:],
                                                       op0=ALU.mult, op1=ALU.mult).then_inc(ln_t, 1)
                    if k > 1:
                        dve.wait_ge(ln_hi, KC * l + k - 1)
                        split_lo(hA_lo[:, k - 2, :], work[:, k - 2, :], hA_hi[:, k - 2, :]).then_inc(ln_lo, 1)
                for i in range(4):
                    dve.wait_ge(panel_done, base + M_CO + i + 1)
                    dve.wait_ge(gates_done, 2 * l + 2)
                    nc.vector.tensor_tensor(tmp_a[:], pair(4 + i % 2), gates[:, 8 + 2 * i:10 + 2 * i, :],
                                            ALU.mult).then_inc(yc_done, 1)
                    dve.wait_ge(yc_done, 4 * l + i + 1)
                    if i > 0:
                        dve.wait_ge(y_lo_done, 4 * l + i)
                    nc.vector.tensor_tensor(tmp_b[:], tmp_a[:], y_attn[:, 2 * i:2 * i + 2, :], ALU.add).then_inc(y_done, 1)
                    dve.wait_ge(y_hi_done, 4 * l + i + 1)
                    split_lo(hB_lo[:, 2 * i:2 * i + 2, :], tmp_b[:], hB_hi[:, 2 * i:2 * i + 2, :]).then_inc(y_lo_done, 1)
                    lo(base + M_CO + i + RING)
                g = 3 * l + 1
                dve.wait_ge(gate_done, g + 1)
                for i in range(4):
                    dve.wait_ge(panel_done, base + M_WO + i + 1)
                    for o in (2 * i, 2 * i + 1):
                        nc.vector.scalar_tensor_tensor(out=x[:, o, :], in0=pair(i)[:, o % 2, :], scalar=gate[:, g, o:o + 1],
                                                       in1=x[:, o, :], op0=ALU.mult, op1=ALU.add).then_inc(x_done, 1)
                    if i < 3:
                        lo(base + M_WO + i + RING)

            def first_unit(n, k, src, a, b):
                if n:
                    dve.wait_ge(ada_step, n)
                nc.vector.scalar_tensor_tensor(out=ada_acc[0][:, a:b], in0=src, scalar=c_act[:, k:k + 1],
                                               in1=ada_acc[0][:, a:b], op0=ALU.mult, op1=ALU.add).then_inc(ada_step, 1)

            def first_group():
                for k in range(KC):
                    dve.wait_ge(first_in[k % 4], 16 * (k // 4 + 1))
                    first_unit(k, k, first_raw[k % 4], 0, 2 * D)

            def first_gate():
                for k in range(KC):
                    if k % 2 == 0:
                        dve.wait_ge(first_in[k // 2], 16 * 3)
                    first_unit(KC + k, k, first_raw[k // 2][:, (k % 2) * D:(k % 2 + 1) * D], 2 * D, GW)

            nc.vector.memset(ones[:], 1.0).then_inc(setup_done, 1)
            nc.vector.memset(zeros[:], 0.0).then_inc(setup_done, 1)
            nc.vector.memset(eps[:], EPS).then_inc(setup_done, 1)
            nc.vector.memset(conv_in[:], 0.0).then_inc(setup_done, 1)
            dve.wait_ge(cleared, 1)
            dve.wait_ge(c_ready, 1)
            first_group()
            lo(0)
            for b in range(4):
                reduce_turned(b, (B_ADA, B_U)[b % 2], 0, b)
            add_bias(0, 4, 0, 0, 2 * KC)
            finish_gain(0)
            for l in range(DEPTH):
                ffn(2 * l)
                mix(l)
                ffn(2 * l + 1)
            norm(3 * DEPTH)


def kernel(**inputs):
    import numpy as np
    import concourse.bacc as bacc
    from concourse.bass_utils import run_bass_kernel_spmd

    def columns(a):
        a = np.asarray(a)
        n = a.shape[-1] // P
        return a.reshape(-1, n, P).transpose(2, 0, 1).reshape(P, -1)

    a = {k: np.asarray(v) for k, v in inputs.items()}
    parts = [columns(a["c"]), columns(a["final_g"])]
    for l in range(DEPTH):
        taps = a["conv_w"][l].reshape(TAPS, KC, P).transpose(2, 1, 0).reshape(P, KC * TAPS)
        parts += [columns(a["ada_b"][l]), columns(a["norm_g"][l]), taps, columns(a["conv_b"][l]),
                  columns(a["conv_ln_g"][l]), columns(a["conv_ln_b"][l])]
    params = np.concatenate(parts, axis=1)
    xT = a["x"].reshape(T, KC, P).transpose(2, 1, 0)

    import ml_dtypes
    half = HD // 2
    inv_freq = (np.float32(10000.0) ** (-(np.arange(half, dtype=np.float32) * np.float32(2.0) / np.float32(HD)))).astype(np.float32)
    ang = np.arange(T, dtype=np.float32)[None, :] * inv_freq[:, None]
    rows = np.arange(P) % half
    rope = np.stack([np.cos(ang)[rows], np.sin(ang)[rows]], axis=1).astype(np.float32)
    perm = np.zeros((P, 2, P), np.float32)
    for r in range(P):
        if r % HD < half:
            perm[r + half, 0, r] = -1.0
        else:
            perm[r - half, 0, r] = 1.0
        perm[r, 1, r] = 1.0
    mask = np.zeros((P, TT, NG, T), np.float32)
    dist = (np.arange(T).reshape(TT, P).T)[:, :, None] - np.arange(T)[None, None, :]
    for g in range(NG):
        ok = (dist >= 0) & (dist <= WINDOW[g]) & (dist % DILATION[g] == 0)
        mask[:, :, g, :] = np.where(ok, 0.0, -1e30)
    arrays = {
        "xT": xT, "params": params, "rope": rope, "perm": perm, "mask": mask.astype(ml_dtypes.bfloat16),
        "ada_w": a["ada_w"], "ffn_wg": a["ffn_wg"], "ffn_wu": a["ffn_wu"], "ffn_wd": a["ffn_wd"], "w_in": a["w_in"],
        "attn_wo": a["attn_wo"], "conv_wo": a["conv_wo"], "w_out": a["w_out"],
    }
    nc = bacc.Bacc("TRN2", target_bir_lowering=False, num_devices=1)
    arrays = {f"in_{k}": np.ascontiguousarray(v) for k, v in arrays.items()}
    args = [nc.dram_tensor(k, v.shape, mybir.dt.from_np(v.dtype), kind="ExternalInput").ap() for k, v in arrays.items()]
    out = nc.dram_tensor("out_T", (P, KC, T), F32, kind="ExternalOutput").ap()
    decoder_program(nc, *args, out)
    r = run_bass_kernel_spmd(nc, [arrays], core_ids=[0])
    got = r.results[0]["out_T"]
    return got.transpose(2, 1, 0).reshape(1, T, D)
```

```python
from contextlib import ExitStack

import concourse.bass as bass
from concourse import mybir

ALU = mybir.AluOpType
ACT = mybir.ActivationFunctionType
AX = mybir.AxisListType
F32 = mybir.dt.float32
F32R = mybir.dt.float32r
BF16 = mybir.dt.bfloat16

P = 128
D = 1024
T = 256
DEPTH = 2
KC = D // P
TT = T // P
FF = 2816
FB = FF // 256
HD = 64
HPG = 4
NG = 3
DILATION = (1, 4, 16)
WINDOW = (128, 512, 2048)
TAPS = 31
PAD = TAPS - 1
GROUPS = 3 * DEPTH
GW = 3 * D
EPS = 1e-6
PW = KC * 256
RING = 3

FFN_PANELS = 3 * FB
M_U, M_QK, M_GA0, M_V, M_G, M_AO, M_CO, M_WO = 0, 8, 14, 15, 18, 25, 26, 30
MIX_PANELS = 34
LAYER_PANELS = 2 * FFN_PANELS + MIX_PANELS
PANELS = DEPTH * LAYER_PANELS
QUOTAS = (0, 12, 14, 12, 10, 11, 10, 8, 14, 14, 8, 8, 8, 8, 8, 6, 9, 9, 9, 14, 9, 14, 9, 8, 10)
WHOLE = (4, 7, 10, 12, 15, 18, 20, 22)


def is_whole(p):
    return p % LAYER_PANELS - FFN_PANELS in WHOLE


def splits(p):
    l, i = divmod(p, LAYER_PANELS)
    return p + 1 - l * len(WHOLE) - sum(w <= i - FFN_PANELS for w in WHOLE)

C_C = 0
C_FG = C_C + KC
C_LAYER = C_FG + KC
L_ADAB, L_NG, L_CW = 0, 9 * KC, 12 * KC
L_CB = L_CW + TAPS * KC
L_LG, L_LB = L_CB + KC, L_CB + 2 * KC
L_W = L_CB + 3 * KC
NPAR = C_LAYER + DEPTH * L_W


def col(layer, which, n=0):
    return C_LAYER + layer * L_W + which + n


def decoder_program(nc, xT, params, rope, perm, mask, ada_w, ffn_wg, ffn_wu, ffn_wd, w_in, attn_wo, conv_wo, w_out, out):
    with ExitStack() as ctx:
        def sb(name, shape, dt=F32):
            return ctx.enter_context(nc.sbuf_tensor(name, shape, dt))

        def sem(name):
            return ctx.enter_context(nc.semaphore(name))

        raw = sb("raw", [P, RING, PW])
        w_hi = sb("w_hi", [P, RING, PW], F32R)
        w_lo = sb("w_lo", [P, RING, PW], F32R)
        x = sb("x", [P, KC, T])
        work = sb("work", [P, KC, T])
        hA_hi = sb("hA_hi", [P, KC, T], F32R)
        hA_lo = sb("hA_lo", [P, KC, T], F32R)
        hB_hi = sb("hB_hi", [P, KC, T], F32R)
        hB_lo = sb("hB_lo", [P, KC, T], F32R)
        conv_in = sb("conv_in", [P, KC, PAD + T])
        v_sb = sb("v_sb", [P, TT, NG * 256])
        tmp_a = sb("tmp_a", [P, 2, T])
        tmp_b = sb("tmp_b", [P, 2, T])
        mid_hi = sb("mid_hi", [P, 2, T], F32R)
        mid_lo = sb("mid_lo", [P, 2, T], F32R)
        mask_sb = sb("mask_sb", [P, TT, NG, T], BF16)
        rope_sb = sb("rope_sb", [P, 2, T])
        perm_sb = sb("perm_sb", [P, 2, P])
        par = sb("par", [P, NPAR])
        ones = sb("ones", [P, P])
        zeros = sb("zeros", [P, 512], BF16)
        c_act = sb("c_act", [P, KC])
        mods = sb("mods", [P, GROUPS, 3 * KC])
        gs = sb("gs", [P, GROUPS, KC])
        gate = sb("gate", [P, GROUPS, KC])
        std = sb("std", [P, T])
        rstd = sb("rstd", [P, T])
        eps = sb("eps", [P, 1])
        spare = sb("spare", [P, 1])
        negmax = sb("negmax", [P, 2 * HPG])
        den = sb("den", [P, 2 * HPG])
        rden = sb("rden", [P, 2 * HPG])
        arena = sb("arena", [P, 4 * GW])
        ada_raw = [arena[:, i * GW:(i + 1) * GW] for i in range(2)]
        ada_acc = [arena[:, (2 + i) * GW:(3 + i) * GW] for i in range(2)]
        gates = arena[:, 0:16 * T].rearrange("p (c t) -> p c t", t=T)
        y_attn = arena[:, 16 * T:24 * T].rearrange("p (c t) -> p c t", t=T)
        h_whole = y_attn
        first_raw = [arena[:, i * 2 * D:(i + 1) * 2 * D] for i in (0, 1, 2)] + [arena[:, 3 * GW:3 * GW + 2 * D]]
        o = 24 * T
        qk = arena[:, o:o + 12 * T].rearrange("p (g w c t) -> p g w c t", g=NG, w=2, t=T)
        o += 12 * T
        probs = [arena[:, o + 3 * T:o + 3 * T + 3 * P].rearrange("p (g t) -> p g t", g=NG),
                 arena[:, o:o + 3 * T].rearrange("p (g t) -> p g t", g=NG)]
        o += 3 * T + 3 * P
        probsT = arena[:, o:o + 6 * T].rearrange("p (g k t) -> p g k t", g=NG, k=TT)
        assert o + 6 * T <= 4 * GW

        ps = ctx.enter_context(nc.psum_tensor("ps", [P, 8, 512], F32))
        B_G, B_U, B_STAT, B_ADA = 4, 5, 6, 7
        KBANK = (3, 4, 5)
        S1 = ps[:, 0:2, :].rearrange("p b n -> p (b n)")[:, 0:NG * T].rearrange("p (g t) -> p g t", g=NG)
        S0 = ps[:, 2, 0:NG * P].rearrange("p (g t) -> p g t", g=NG)
        T1 = ps[:, 0:2, :].rearrange("p b n -> p (b n)")[:, 0:6 * P].rearrange("p (g k t) -> p g k t", g=NG, k=TT)
        T0 = S0

        def pair(bank):
            return ps[:, bank, :].rearrange("p (c t) -> p c t", t=T)

        def acc(o):
            return ps[:, o // 2, (o % 2) * T:(o % 2 + 1) * T]

        consts_in = sem("consts_in")
        tables_in = sem("tables_in")
        masks_in = sem("masks_in")
        x_in = sem("x_in")
        first_in = [sem(f"first_in{i}") for i in range(4)]
        raw_in = [sem(f"raw_in{i}") for i in range(RING)]
        ada_in = [sem(f"ada_in{i}") for i in range(2)]
        out_done = sem("out_done")
        setup_done = sem("setup_done")
        c_ready = sem("c_ready")
        hi_done, lo_done, panel_done = sem("hi_done"), sem("lo_done"), sem("panel_done")
        ada_step, mods_done, mods_step = sem("ada_step"), sem("mods_done"), sem("mods_step")
        ada_turned, ada_reduced = sem("ada_turned"), sem("ada_reduced")
        sq_done, ssq_done, std_done, rstd_done = sem("sq_done"), sem("ssq_done"), sem("std_done"), sem("rstd_done")
        t_done, h_hi_done, h_lo_done = sem("t_done"), sem("h_hi_done"), sem("h_lo_done")
        silu_done, mid_done, mid_hi_done, mid_lo_done = sem("silu_done"), sem("mid_done"), sem("mid_hi_done"), sem("mid_lo_done")
        acc_done, x_done = sem("acc_done"), sem("x_done")
        evac_done, glu_done, conv_step = sem("evac_done"), sem("glu_done"), sem("conv_step")
        rot_done, rope_mul, rope_done = sem("rot_done"), sem("rope_mul"), sem("rope_done")
        score_done, masked_done, max_done, exp_done = sem("score_done"), sem("masked_done"), sem("max_done"), sem("exp_done")
        rden_done, prob_done, turn_done, probT_done = sem("rden_done"), sem("prob_done"), sem("turn_done"), sem("probT_done")
        pv_done, o_hi_done, o_lo_done = sem("pv_done"), sem("o_hi_done"), sem("o_lo_done")
        gates_done = sem("gates_done")
        h_whole_done = sem("h_whole_done")
        ln_sum, xc_done, ln_sq, ln_std, ln_rstd = sem("ln_sum"), sem("xc_done"), sem("ln_sq"), sem("ln_std"), sem("ln_rstd")
        ln_t, ln_silu, ln_hi, ln_lo = sem("ln_t"), sem("ln_silu"), sem("ln_hi"), sem("ln_lo")
        ao_done, ya_done, yc_done, y_done, y_hi_done, y_lo_done = (
            sem("ao_done"), sem("ya_done"), sem("yc_done"), sem("y_done"), sem("y_hi_done"), sem("y_lo_done"))
        final_done = sem("final_done")
        cleared = sem("cleared")
        gate_done = sem("gate_done")

        wg_v = ffn_wg.rearrange("l f (k p) n -> l f p k n", p=P)
        wu_v = ffn_wu.rearrange("l f (k p) n -> l f p k n", p=P)
        wd_v = ffn_wd.rearrange("l f (j k p) n -> l f j p k n", k=2, p=P)
        win_v = w_in.rearrange("l (k p) n -> l p k n", p=P)
        ao_v = attn_wo.rearrange("l (k p) n -> l p k n", p=P)
        co_v = conv_wo.rearrange("l (k p) n -> l p k n", p=P)
        wo_v = w_out.rearrange("l (k p) n -> l p k n", p=P)

        def kview(flat):
            return flat.rearrange("p (k n) -> p k n", k=KC)

        def dview(flat):
            return flat.rearrange("p (k n) -> p k n", k=2)

        QKV = NG * 256
        U0, GA0 = 3 * QKV, 3 * QKV + 2 * D
        win_cols = []
        for i in range(4):
            win_cols += [U0 + 256 * i, U0 + D + 256 * i]
        for g in range(NG):
            win_cols += [256 * g, QKV + 256 * g]
        win_cols += [GA0]
        win_cols += [2 * QKV + 256 * g for g in range(NG)]
        win_cols += [GA0 + 256 * i for i in range(1, 8)]

        def ffn_base(f):
            return (f // 2) * LAYER_PANELS + (f % 2) * (FFN_PANELS + MIX_PANELS)

        def mix_base(l):
            return l * LAYER_PANELS + FFN_PANELS

        H = KC // 2
        ADA_PLAN = (((0, KC, ((0, 1, 0), (1, 2, 0))),),
                    ((0, H, ((0, 3, 0), (1, 4, 0))), (H, KC, ((0, 3, 0),))),
                    ((0, H, ((0, 5, 0), (1, 4, H))), (H, KC, ((0, 5, 0),))),
                    ())

        def ada_sequence(f):
            return [(ph, i, slot, g, j + shift) for ph, (first, last, units) in enumerate(ADA_PLAN[f])
                    for j in range(first, last) for i, (slot, g, shift) in enumerate(units)]

        def ada_units(f):
            return len(ada_sequence(f))

        def ada_until(f, g):
            return max(n + 1 for n, u in enumerate(ada_sequence(f)) if u[3] == g)

        def ada_free(f, ph, i):
            seq = ada_sequence(f)
            slots = [u[2] for u in seq]
            behind = []
            for n, u in enumerate(seq):
                if u[:2] == (ph, i):
                    m = n - 1
                    while m >= 0 and slots[m] != slots[n]:
                        m -= 1
                    behind += [n - m] if m >= 0 else []
            first, _, units = ADA_PLAN[f][ph]
            start = [u[0] for u in seq].index(ph)
            return ada_before(f) + start + i - first * len(units) + 1 - min(behind)

        def ada_before(f):
            return 2 * KC + sum(ada_units(e) for e in range(f))

        ADA_BANKS = (7, 6, 7, 6, 7, 6, 7, 4, 5, 7, 4, 5)

        def ada_batches(f):
            return 6 + (f // 2) * 18 + (f % 2) * 12

        def ada_groups(f):
            return sorted((g, slot) for _, _, slot, g, k in ada_sequence(f) if k == KC - 1)

        def ada_clears(f):
            return [slot for _, _, slot, _, k in ada_sequence(f) if k == 0]

        block = ctx.enter_context(nc.Block())

        @block.sync
        def _(sp):
            def load(p, dst_view, src):
                slot = p % RING
                if is_whole(p - RING):
                    sp.wait_ge(panel_done, p - RING + 1)
                elif p >= RING:
                    sp.wait_ge(lo_done, splits(p - RING))
                sp.dma_start(dst_view(raw[:, slot, :]), src).then_inc(raw_in[slot], 16)

            sp.dma_start(par[:], params).then_inc(consts_in, 16)
            for k in range(KC):
                if k >= 4:
                    sp.wait_ge(ada_step, k - 3)
                sp.dma_start(first_raw[k % 4], ada_w[0, k * P:(k + 1) * P, 0:2 * D]).then_inc(first_in[k % 4], 16)
                if k == 2:
                    sp.dma_start(x[:], xT).then_inc(x_in, 16)
                    sp.dma_start(perm_sb[:], perm).then_inc(tables_in, 16)
            load(0, kview, wg_v[0, 0, :, :, 0:256])
            load(1, kview, wu_v[0, 0, :, :, 0:256])
            load(2, kview, wg_v[0, 0, :, :, 256:512])
            for k in range(4):
                sp.wait_ge(ada_step, 5 + k)
                sp.dma_start(first_raw[k].rearrange("p (r n) -> p r n", r=2),
                             ada_w[0, 2 * k * P:2 * (k + 1) * P, 2 * D:GW].rearrange("(r p) n -> p r n", p=P)
                             ).then_inc(first_in[k], 16)
            sp.dma_start(rope_sb[:], rope).then_inc(masks_in, 16)
            sp.dma_start(mask_sb[:], mask).then_inc(masks_in, 16)

            def ffn(f):
                l, s = f // 2, f % 2
                base = ffn_base(f)
                if f > 0:
                    load(base, kview, wg_v[l, s, :, :, 0:256])
                    load(base + 1, kview, wu_v[l, s, :, :, 0:256])
                else:
                    load(3, kview, wu_v[l, s, :, :, 256:512])
                    load(4, dview, wd_v[l, s, 0])
                with sp.Fori(0 if f else 1, FB - 1) as j:
                    p = base + 2
                    for i, (view, src) in enumerate((
                            (kview, wg_v[l, s, :, :, bass.ds(j * 256 + 256, 256)]),
                            (kview, wu_v[l, s, :, :, bass.ds(j * 256 + 256, 256)]),
                            (dview, wd_v[l, s, bass.ds(j, 1)].rearrange("o p k n -> (o p) k n")))):
                        slot = (p + i) % RING
                        sp.wait_ge(lo_done, j * 3 + splits(p + i - RING))
                        sp.dma_start(view(raw[:, slot, :]), src).then_inc(raw_in[slot], 16)
                load(base + FFN_PANELS - 1, dview, wd_v[l, s, FB - 1])

            def mix(l):
                base = mix_base(l)
                for i, c in enumerate(win_cols):
                    load(base + i, kview, win_v[l, :, :, c:c + 256])
                load(base + M_AO, dview, ao_v[l])
                for i in range(4):
                    load(base + M_CO + i, kview, co_v[l, :, :, 256 * i:256 * i + 256])
                for i in range(4):
                    load(base + M_WO + i, kview, wo_v[l, :, :, 256 * i:256 * i + 256])

            for l in range(DEPTH):
                ffn(2 * l)
                mix(l)
                ffn(2 * l + 1)
            for k in range(KC):
                sp.wait_ge(final_done, k + 1)
                sp.dma_start(out[:, k, :], work[:, k, :]).then_inc(out_done, 16)
            sp.wait_ge(out_done, 16 * KC)

        @block.gpsimd
        def _(pool):
            nc.gpsimd.memset(ada_acc[0], 0.0).then_inc(cleared, 1)
            for f in range(2 * DEPTH):
                if not ADA_PLAN[f]:
                    continue
                if f % 2 == 1:
                    pool.wait_ge(x_done, KC * (3 * (f // 2) + 2))

                def load(slot, g, tile):
                    src = ada_w[g // 3].rearrange("(k p) n -> k p n", p=P)[tile, :, (g % 3) * GW:(g % 3 + 1) * GW]
                    pool.dma_start(ada_raw[slot], src.rearrange("o p n -> (o p) n")).then_inc(ada_in[slot], 16)

                for i, (slot, g, tile) in enumerate(ADA_PLAN[f][0][2]):
                    pool.wait_ge(ada_step, ada_before(f) + (2 * i - 4 if f == 0 else 0))
                    load(slot, g, bass.ds(tile, 1))
                pool.wait_ge(mods_step, 2 + sum(len(ada_groups(e)) for e in range(f)))
                for slot in ada_clears(f):
                    nc.gpsimd.memset(ada_acc[slot], 0.0).then_inc(cleared, 1)
                for ph, (first, last, units) in enumerate(ADA_PLAN[f]):
                    with pool.Fori(max(first, 1), last) as j:
                        for i, (slot, g, shift) in enumerate(units):
                            pool.wait_ge(ada_step, j * len(units) + ada_free(f, ph, i))
                            load(slot, g, bass.ds(j + shift, 1) if shift else bass.ds(j, 1))

        @block.tensor
        def _(pe):
            def three(out_ap, stat, mov, start, stop, **kw):
                nc.tensor.matmul(out_ap, stat[0], mov[0], start=start, stop=False, **kw)
                nc.tensor.matmul(out_ap, stat[0], mov[1], start=False, stop=False, **kw)
                return nc.tensor.matmul(out_ap, stat[1], mov[0], start=False, stop=stop, **kw)

            def k_panel(slot, rhs, bank, h_wait=None, between=None):
                hi, lo = kview(w_hi[:, slot, :]), kview(w_lo[:, slot, :])

                def tile(t, k, **kw):
                    c = slice(t * P, (t + 1) * P)
                    return three(pair(bank)[:, t, :], (hi[:, k, c], lo[:, k, c]), (rhs[0][:, k, :], rhs[1][:, k, :]),
                                 k == 0 and not (kw and t), k == KC - 1, **kw)

                if h_wait is None:
                    for t in range(2):
                        if t and between:
                            between()
                        for k in range(KC):
                            mm = tile(t, k)
                else:
                    for k in range(KC):
                        h_wait(k)
                        for t in range(2):
                            mm = tile(t, k, skip_group_check=True)
                mm.then_inc(panel_done, 1)

            def split_ready(p):
                pe.wait_ge(hi_done, splits(p))
                pe.wait_ge(lo_done, splits(p))

            def whole_panel(slot, bank, between=None):
                w = kview(raw[:, slot, :])
                for t in range(2):
                    if t and between:
                        between()
                    for k in range(KC):
                        mm = nc.tensor.matmul(pair(bank)[:, t, :], w[:, k, t * P:(t + 1) * P], h_whole[:, k, :],
                                              start=(k == 0), stop=(k == KC - 1))
                mm.then_inc(panel_done, 1)

            hA = (hA_hi, hA_lo)
            hB = (hB_hi, hB_lo)

            def column_sums(n_sem, done_sem, base, src):
                for k in range(KC):
                    pe.wait_ge(n_sem, base + k + 1)
                    mm = nc.tensor.matmul(ps[:, B_STAT, 0:T], ones[:], src(k), start=(k == 0), stop=(k == KC - 1))
                mm.then_inc(done_sem, 1)

            def square_sums(n, first, last):
                for k in range(first, last):
                    pe.wait_ge(sq_done, KC * n + k + 1)
                    mm = nc.tensor.matmul(ps[:, B_STAT, 0:T], ones[:], work[:, k, :], start=(k == 0), stop=(k == KC - 1))
                if last == KC:
                    mm.then_inc(ssq_done, 1)

            def ada_turn(m, bank, units, which, b):
                pe.wait_ge(ada_step, units)
                if m >= 2:
                    pe.wait_ge(ada_reduced, m - 1)
                for i in range(4):
                    c = 4 * b + i
                    mm = nc.tensor.transpose(ps[:, bank, i * P:(i + 1) * P], ada_acc[which][:, c * P:(c + 1) * P],
                                             perm_sb[:, 1, :])
                mm.then_inc(ada_turned, 1)

            def d_panel(slot, j_last=False, between=None):
                hi, lo = dview(w_hi[:, slot, :]), dview(w_lo[:, slot, :])
                if not j_last:
                    for kk in range(2):
                        for o in range(KC):
                            c = slice(o * P, (o + 1) * P)
                            mm = three(acc(o), (hi[:, kk, c], lo[:, kk, c]), (mid_hi[:, kk, :], mid_lo[:, kk, :]),
                                       False, False, skip_group_check=True)
                    mm.then_inc(panel_done, 1)
                else:
                    for o in range(KC):
                        for kk in range(2):
                            c = slice(o * P, (o + 1) * P)
                            mm = three(acc(o), (hi[:, kk, c], lo[:, kk, c]), (hB_hi[:, kk, :], hB_lo[:, kk, :]),
                                       False, kk == 1, skip_group_check=True)
                        if o % 2 == 1:
                            mm.then_inc(acc_done if o < KC - 1 else panel_done, 1)
                            between(o // 2)

            def ffn(f):
                base = ffn_base(f)
                n = 3 * (f // 2) + 2 * (f % 2)
                if f > 0:
                    pe.wait_ge(x_done, KC * n)
                for b in range(4):
                    nc.tensor.matmul(ps[:, b, :], zeros[:, 0:P], zeros[:, :], start=True, stop=False,
                                     skip_group_check=True)
                split_ready(base)
                k_panel(base % RING, hA, B_G, lambda k: pe.wait_ge(h_lo_done, KC * n + k + 1))
                split_ready(base + 1)
                k_panel((base + 1) % RING, hA, B_U)
                if f == 0:
                    for b in (4, 5):
                        ada_turn(b, (B_ADA, B_STAT)[b % 2], 2 * KC, 0, b)
                with pe.Fori(0, FB - 2) as j:
                    p = base + 2
                    pe.wait_ge(hi_done, j * 3 + splits(p))
                    pe.wait_ge(lo_done, j * 3 + splits(p))
                    pe.wait_ge(silu_done, j + (f * FB + 1))
                    k_panel(p % RING, hA, B_G)
                    pe.wait_ge(hi_done, j * 3 + splits(p + 1))
                    pe.wait_ge(lo_done, j * 3 + splits(p + 1))
                    pe.wait_ge(mid_done, j + (f * FB + 1))
                    k_panel((p + 1) % RING, hA, B_U)
                    pe.wait_ge(hi_done, j * 3 + splits(p + 2))
                    pe.wait_ge(lo_done, j * 3 + splits(p + 2))
                    pe.wait_ge(mid_lo_done, j + (f * FB + 1))
                    d_panel((p + 2) % RING)
                nb = 6 * len(ada_groups(f))

                def turns(*which):
                    for i in which:
                        if i < nb:
                            g, slot = ada_groups(f)[i // 6]
                            ada_turn(ada_batches(f) + i, ADA_BANKS[i], ada_before(f) + ada_until(f, g), slot, i % 6)

                p = base + 2 + 3 * (FB - 2)
                turns(0, 1)
                split_ready(p)
                pe.wait_ge(silu_done, f * FB + FB - 1)
                k_panel(p % RING, hA, B_G)
                turns(2, 3)
                split_ready(p + 1)
                pe.wait_ge(mid_done, f * FB + FB - 1)
                k_panel((p + 1) % RING, hA, B_U)
                turns(4, 5)
                split_ready(p + 2)
                pe.wait_ge(mid_lo_done, f * FB + FB - 1)
                d_panel((p + 2) % RING)
                split_ready(p + 3)
                pe.wait_ge(mid_lo_done, f * FB + FB)
                turns(6, 7)

                def between(i):
                    if i == 0:
                        turns(8, 9)
                    elif i == 1:
                        turns(10, 11)
                    elif i == 2:
                        square_sums(n + 1, 0, 2)
                    else:
                        square_sums(n + 1, 2, KC)

                d_panel((p + 3) % RING, True, between)

            def mix(l):
                base = mix_base(l)
                e0 = 25 * l

                n = 3 * l + 1
                for i in range(RING):
                    split_ready(base + i)
                    k_panel((base + i) % RING, hA, KBANK[(base + i) % RING],
                            (lambda k: pe.wait_ge(h_lo_done, KC * n + k + 1)) if i == 0 else None)
                pe.wait_ge(h_whole_done, l + 1)
                with pe.Fori(0, 3) as j:
                    for i in range(RING):
                        q = base + RING + i
                        pe.wait_ge(evac_done, j * RING + (e0 + i + 1))
                        if is_whole(q):
                            pe.wait_ge(raw_in[q % RING], j * 16 + 16 * (q // RING + 1))
                            whole_panel(q % RING, KBANK[q % RING])
                        else:
                            pe.wait_ge(hi_done, j * (splits(q + RING) - splits(q)) + splits(q))
                            pe.wait_ge(lo_done, j * (splits(q + RING) - splits(q)) + splits(q))
                            k_panel(q % RING, hA, KBANK[q % RING])

                def v_panel(g):
                    p = base + M_V + g
                    slot = p % RING
                    pe.wait_ge(evac_done, e0 + M_V + g - RING + 1)
                    if is_whole(p):
                        pe.wait_ge(raw_in[slot], 16 * (p // RING + 1))
                        w = kview(raw[:, slot, :])
                        for t in range(TT):
                            for k in range(KC):
                                mm = nc.tensor.matmul(pair(KBANK[slot])[:, t, :], h_whole[:, k, t * P:(t + 1) * P],
                                                      w[:, k, :], start=(k == 0), stop=(k == KC - 1))
                        mm.then_inc(panel_done, 1)
                        return
                    split_ready(p)
                    hi, lo = kview(w_hi[:, slot, :]), kview(w_lo[:, slot, :])
                    for t in range(TT):
                        c = slice(t * P, (t + 1) * P)
                        for k in range(KC):
                            mm = three(pair(KBANK[slot])[:, t, :], (hA_hi[:, k, c], hA_lo[:, k, c]),
                                       (hi[:, k, :], lo[:, k, :]), k == 0, k == KC - 1)
                    mm.then_inc(panel_done, 1)

                pe.wait_ge(masks_in, 32)

                def rotate(g):
                    for w in range(2):
                        r = 6 * l + 2 * g + w
                        pe.wait_ge(evac_done, e0 + M_QK + 2 * g + w + 1)
                        if r % 6 >= 2:
                            pe.wait_ge(rope_done, r - 1)
                        for c in range(2):
                            mm = nc.tensor.matmul(pair((2, 7)[w])[:, c, :], perm_sb[:, 0, :], qk[:, g, w, c, :],
                                                  start=True, stop=True)
                        mm.then_inc(rot_done, 1)

                def win_panel(i, between=None):
                    p = base + i
                    pe.wait_ge(evac_done, e0 + i - RING + 1)
                    if is_whole(p):
                        pe.wait_ge(raw_in[p % RING], 16 * (p // RING + 1))
                        whole_panel(p % RING, KBANK[p % RING], between)
                    else:
                        split_ready(p)
                        k_panel(p % RING, hA, KBANK[p % RING], between=between)

                def scores(h):
                    if h == 0:
                        pe.wait_ge(rope_done, 6 * (l + 1))
                    else:
                        pe.wait_ge(probT_done, 2 * (HPG * l + h))
                    for q in range(TT):
                        keys = (q + 1) * P
                        for g in range(NG):
                            head = HPG * g + h
                            part = slice((head % 2) * HD, (head % 2 + 1) * HD)
                            c = (head // 2) % 2
                            dst = S1[:, g, :] if q else S0[:, g, :]
                            mm = nc.tensor.matmul(dst, qk[part, g, 0, c, q * P:(q + 1) * P], qk[part, g, 1, c, 0:keys],
                                                  start=True, stop=True)
                        mm.then_inc(score_done, 1)

                def turn(h):
                    for q in range(TT):
                        pe.wait_ge(prob_done, 2 * (HPG * l + h) + q + 1)
                        for g in range(NG):
                            for k in range(q + 1):
                                dst = T1[:, g, k, :] if q else T0[:, g, :]
                                mm = nc.tensor.transpose(dst, probs[q][:, g, k * P:(k + 1) * P], perm_sb[:, 1, :])
                        mm.then_inc(turn_done, 1)

                def pv(h):
                    pe.wait_ge(probT_done, 2 * (HPG * l + h + 1))
                    half = slice((h % 2) * HD, (h % 2 + 1) * HD)
                    bank = 6 + h // 2
                    for g in range(NG):
                        cols = slice((HPG * g + h) * HD, (HPG * g + h + 1) * HD)
                        nc.tensor.matmul(ps[half, bank, 0:T], v_sb[:, 0, cols], probsT[:, g, 0, :],
                                         start=(g == 0), stop=False)
                        mm = nc.tensor.matmul(ps[half, bank, P:T], v_sb[:, 1, cols], probsT[:, g, 1, P:T],
                                              start=False, stop=(g == NG - 1))
                    mm.then_inc(pv_done, 1)

                win_panel(M_QK + 4)
                rotate(0)
                win_panel(M_QK + 5)
                win_panel(M_GA0)
                rotate(1)
                v_panel(0)
                rotate(2)
                v_panel(1)
                scores(0)
                v_panel(2)
                turn(0)
                for h in range(1, HPG):
                    win_panel(M_G + 2 * h - 2)
                    pv(h - 1)
                    scores(h)
                    win_panel(M_G + 2 * h - 1)
                    turn(h)
                win_panel(M_G + 6, lambda: pv(3))

                def attention_out(first, last):
                    p = base + M_AO
                    hi, lo = dview(w_hi[:, p % RING, :]), dview(w_lo[:, p % RING, :])
                    for i in range(first, last):
                        if i == 3:
                            pe.wait_ge(evac_done, e0 + 25)
                        for t in range(2):
                            c = slice((2 * i + t) * P, (2 * i + t + 1) * P)
                            for kk in range(2):
                                mm = three(pair(i)[:, t, :], (hi[:, kk, c], lo[:, kk, c]),
                                           (mid_hi[:, kk, :], mid_lo[:, kk, :]), kk == 0, kk == 1)
                        mm.then_inc(ao_done if i < 3 else panel_done, 1)

                def conv_sums(first, last):
                    pe.wait_ge(conv_step, KC * TAPS * l + last * TAPS)
                    for k in range(first, last):
                        mm = nc.tensor.matmul(ps[:, B_STAT, 0:T], ones[:], work[:, k, :], start=(k == 0),
                                              stop=(k == KC - 1))
                    return mm

                conv_sums(0, 6)
                conv_sums(6, KC).then_inc(ln_sum, 1)
                split_ready(base + M_AO)
                pe.wait_ge(o_lo_done, 2 * (l + 1))
                attention_out(0, 2)
                pe.wait_ge(xc_done, KC * (l + 1))
                column_sums(ln_sq, ln_sum, KC * l, lambda k: conv_in[:, k, PAD:])
                attention_out(2, 4)

                for i in range(4):
                    p = base + M_CO + i
                    split_ready(p)
                    if i >= 2:
                        pe.wait_ge(yc_done, 4 * l + i - 1)
                    else:
                        pe.wait_ge(evac_done, e0 + 25)
                    if i == 0:
                        k_panel(p % RING, hA, 4 + i % 2, lambda k: pe.wait_ge(ln_lo, KC * l + k + 1))
                    else:
                        k_panel(p % RING, hA, 4 + i % 2)
                for i in range(4):
                    p = base + M_WO + i
                    split_ready(p)
                    pe.wait_ge(ya_done, 4 * l + i + 1)
                    k_panel(p % RING, hB, i, (lambda k: pe.wait_ge(y_lo_done, 4 * l + k // 2 + 1)) if i == 0 else None)
                    if i >= 1:
                        square_sums(3 * l + 2, 2 * (i - 1), 2 * i)
                square_sums(3 * l + 2, 6, KC)

            pe.wait_ge(setup_done, 4)
            pe.wait_ge(tables_in, 16)
            square_sums(0, 0, KC)
            for b in range(4):
                ada_turn(b, (B_ADA, B_U)[b % 2], KC, 0, b)
            for l in range(DEPTH):
                ffn(2 * l)
                mix(l)
                ffn(2 * l + 1)

        @block.scalar
        def _(act):
            def hi(p):
                slot = p % RING
                if is_whole(p):
                    return
                act.wait_ge(raw_in[slot], 16 * (p // RING + 1))
                if p >= RING:
                    act.wait_ge(panel_done, p - RING + 1)
                nc.scalar.copy(w_hi[:, slot, :], raw[:, slot, :]).then_inc(hi_done, 1)

            def hi_loop(j, p):
                slot = p % RING
                act.wait_ge(raw_in[slot], j * 16 + 16 * (p // RING + 1))
                act.wait_ge(panel_done, j * 3 + (p - RING + 1))
                nc.scalar.copy(w_hi[:, slot, :], raw[:, slot, :]).then_inc(hi_done, 1)

            def preload(func):
                nc.scalar.activation(spare[:], eps[:], func)

            def squares(n, first, last):
                for k in range(first, last):
                    if n > 0:
                        act.wait_ge(x_done, KC * (n - 1) + k + 1)
                    nc.scalar.activation(work[:, k, :], x[:, k, :], ACT.Square).then_inc(sq_done, 1)

            def norm(n):
                if n % 3 == 2:
                    squares(n, KC - 2, KC)
                else:
                    preload(ACT.Sqrt)
                    if n == 0:
                        act.wait_ge(x_in, 16)
                    squares(n, 0, KC)
                act.wait_ge(ssq_done, n + 1)
                nc.scalar.activation(std[:], ps[:, B_STAT, 0:T], ACT.Sqrt, bias=eps[:, 0:1],
                                     scale=1.0 / D).then_inc(std_done, 1)
                if n == 3 * DEPTH:
                    return
                preload(ACT.Sigmoid if n % 3 == 1 else ACT.Silu)
                if n == 0:
                    hi(0)
                for k in range(KC):
                    act.wait_ge(t_done, KC * n + k + 1)
                    nc.scalar.activation(hA_hi[:, k, :], work[:, k, :], ACT.Identity,
                                         bias=mods[:, n, k:k + 1]).then_inc(h_hi_done, 1)

            def silu():
                nc.scalar.activation(tmp_a[:], pair(B_G), ACT.Silu).then_inc(silu_done, 1)

            def ffn(f):
                base = ffn_base(f)
                norm(3 * (f // 2) + 2 * (f % 2))
                if f == 0:
                    hi(1)
                hi(base + 2)
                act.wait_ge(panel_done, base + 1)
                silu()
                hi(base + 3)
                hi(base + 4)
                act.wait_ge(mid_done, f * FB + 1)
                nc.scalar.copy(mid_hi[:], tmp_b[:]).then_inc(mid_hi_done, 1)
                last = ffn_base(f) + FFN_PANELS == PANELS
                n = FB - 2
                with act.Fori(0, n) as j:
                    p = base + 2
                    act.wait_ge(panel_done, j * 3 + (p + 1))
                    act.wait_ge(mid_done, j + (f * FB + 1))
                    silu()
                    hi_loop(j, p + 3)
                    hi_loop(j, p + 4)
                    hi_loop(j, p + 5)
                    act.wait_ge(mid_done, j + (f * FB + 2))
                    nc.scalar.copy(mid_hi[:], tmp_b[:]).then_inc(mid_hi_done, 1)
                p = base + 2 + 3 * n
                act.wait_ge(panel_done, p + 1)
                act.wait_ge(mid_done, f * FB + FB - 1)
                silu()
                hi(p + 3)
                act.wait_ge(mid_done, f * FB + FB)
                nc.scalar.copy(hB_hi[:, 0:2, :], tmp_b[:]).then_inc(mid_hi_done, 1)
                if not last:
                    hi(p + 4)
                    hi(p + 5)

            def mix(l):
                base = mix_base(l)
                norm(3 * l + 1)
                hi(base + 2)
                for k in range(KC):
                    op = nc.scalar.activation(h_whole[:, k, :], work[:, k, :], ACT.Identity,
                                              bias=mods[:, 3 * l + 1, k:k + 1])
                op.then_inc(h_whole_done, 1)

                def panel(i, dst, func, src_t=None):
                    act.wait_ge(panel_done, base + i + 1)
                    nc.scalar.activation(dst, pair(KBANK[(base + i) % RING]), func).then_inc(evac_done, 1)
                    hi(base + i + RING)

                for i in range(4):
                    if i:
                        act.wait_ge(glu_done, 4 * l + i)
                    panel(2 * i, tmp_a[:], ACT.Copy)
                    panel(2 * i + 1, tmp_b[:], ACT.Sigmoid)
                for g in range(NG):
                    panel(M_QK + 2 * g, qk[:, g, 0, :, :], ACT.Copy)
                    panel(M_QK + 2 * g + 1, qk[:, g, 1, :, :], ACT.Copy)
                panel(M_GA0, gates[:, 0:2, :], ACT.Copy)
                def v_panel(g):
                    panel(M_V + g, v_sb[:, :, g * 256:(g + 1) * 256], ACT.Copy)

                def gate_panel(i):
                    panel(M_G + i, gates[:, 2 * (i + 1):2 * (i + 2), :], ACT.Copy)

                def exps(h):
                    for q in range(TT):
                        u = 2 * h + q
                        act.wait_ge(max_done, 2 * HPG * l + u + 1)
                        nc.scalar.activation(probs[q], probs[q], ACT.Exp, bias=negmax[:, u:u + 1],
                                             accum_out=den[:, u:u + 1]).then_inc(exp_done, 1)
                    for q in range(TT):
                        u = 2 * h + q
                        act.wait_ge(rden_done, 2 * HPG * l + u + 1)
                        act.wait_ge(exp_done, 2 * HPG * l + u + 1)
                        nc.scalar.activation(probs[q], probs[q], ACT.Copy,
                                             scale=rden[:, u:u + 1]).then_inc(prob_done, 1)

                def turned(h):
                    if h > 0:
                        act.wait_ge(pv_done, HPG * l + h)
                    act.wait_ge(turn_done, 2 * (HPG * l + h) + 1)
                    nc.scalar.copy(probsT[:, :, 0, 0:P], T0).then_inc(probT_done, 1)
                    act.wait_ge(turn_done, 2 * (HPG * l + h) + 2)
                    nc.scalar.copy(probsT[:, :, :, P:T], T1).then_inc(probT_done, 1)

                def head_out(c):
                    act.wait_ge(pv_done, HPG * l + 2 * c + 2)
                    nc.scalar.copy(mid_hi[:, c, :], ps[:, 6 + c, 0:T]).then_inc(o_hi_done, 1)

                v_panel(0)
                v_panel(1)
                exps(0)
                v_panel(2)
                turned(0)
                for h in range(1, HPG):
                    gate_panel(2 * h - 2)
                    exps(h)
                    if h == 2:
                        head_out(0)
                    gate_panel(2 * h - 1)
                    turned(h)
                head_out(1)
                gate_panel(6)
                act.wait_ge(evac_done, 25 * (l + 1))
                nc.scalar.activation(gates[:, 0:8, :], gates[:, 0:8, :], ACT.Sigmoid).then_inc(gates_done, 1)
                nc.scalar.activation(gates[:, 8:16, :], gates[:, 8:16, :], ACT.Sigmoid).then_inc(gates_done, 1)
                preload(ACT.Sqrt)
                for k in range(KC):
                    act.wait_ge(xc_done, KC * l + k + 1)
                    nc.scalar.activation(conv_in[:, k, PAD:], work[:, k, :], ACT.Square).then_inc(ln_sq, 1)
                act.wait_ge(ln_sum, 2 * (l + 1))
                nc.scalar.activation(std[:], ps[:, B_STAT, 0:T], ACT.Sqrt, bias=eps[:, 0:1],
                                     scale=1.0 / D).then_inc(ln_std, 1)
                preload(ACT.Silu)
                for k in range(KC):
                    act.wait_ge(ln_t, KC * l + k + 1)
                    nc.scalar.activation(work[:, k, :], conv_in[:, k, PAD:], ACT.Silu,
                                         bias=par[:, col(l, L_LB, k):col(l, L_LB, k) + 1]).then_inc(ln_silu, 1)
                    act.wait_ge(ln_silu, KC * l + k + 1)
                    nc.scalar.copy(hA_hi[:, k, :], work[:, k, :]).then_inc(ln_hi, 1)
                hi(base + M_AO + RING)
                for i in range(4):
                    hi(base + M_CO + i + RING)
                    act.wait_ge(y_done, 4 * l + i + 1)
                    nc.scalar.copy(hB_hi[:, 2 * i:2 * i + 2, :], tmp_b[:]).then_inc(y_hi_done, 1)
                preload(ACT.Sqrt)
                for i in range(3):
                    hi(base + M_WO + i + RING)
                    squares(3 * l + 2, 2 * i, 2 * i + 2)

            act.wait_ge(consts_in, 16)
            act.wait_ge(setup_done, 4)
            nc.scalar.activation(c_act[:], par[:, C_C:C_C + KC], ACT.Silu).then_inc(c_ready, 1)
            for l in range(DEPTH):
                ffn(2 * l)
                mix(l)
                ffn(2 * l + 1)
            norm(3 * DEPTH)

        @block.vector
        def _(dve):
            def split_lo(dst, whole, hi_part):
                return nc.vector.tensor_tensor(dst, whole, hi_part.bitcast(F32), ALU.subtract)

            def lo(p):
                slot = p % RING
                if is_whole(p):
                    return
                dve.wait_ge(hi_done, splits(p))
                split_lo(w_lo[:, slot, :], raw[:, slot, :], w_hi[:, slot, :]).then_inc(lo_done, 1)

            def lo_loop(j, p):
                slot = p % RING
                dve.wait_ge(hi_done, j * 3 + splits(p))
                split_lo(w_lo[:, slot, :], raw[:, slot, :], w_hi[:, slot, :]).then_inc(lo_done, 1)

            def recip(n, wait, done):
                dve.wait_ge(wait, n + 1)
                nc.vector.reciprocal(rstd[:], std[:]).then_inc(done, 1)
                dve.wait_ge(done, n + 1)

            def norm(n):
                recip(n, std_done, rstd_done)
                if n == 3 * DEPTH:
                    for k in range(KC):
                        nc.vector.scalar_tensor_tensor(out=work[:, k, :], in0=x[:, k, :],
                                                       scalar=par[:, C_FG + k:C_FG + k + 1], in1=rstd[:],
                                                       op0=ALU.mult, op1=ALU.mult).then_inc(final_done, 1)
                    return
                dve.wait_ge(mods_done, n + 1)
                for k in range(KC + 1):
                    if k < KC:
                        nc.vector.scalar_tensor_tensor(out=work[:, k, :], in0=x[:, k, :], scalar=gs[:, n, k:k + 1],
                                                       in1=rstd[:], op0=ALU.mult, op1=ALU.mult).then_inc(t_done, 1)
                    if k > 0:
                        dve.wait_ge(h_hi_done, KC * n + k)
                        dve.wait_ge(t_done, KC * n + k)
                        nc.vector.scalar_tensor_tensor(out=hA_lo[:, k - 1, :], in0=work[:, k - 1, :],
                                                       scalar=mods[:, n, k - 1:k], in1=hA_hi[:, k - 1, :].bitcast(F32),
                                                       op0=ALU.add, op1=ALU.subtract).then_inc(h_lo_done, 1)

            def reduce_turned(m, bank, g, b):
                dve.wait_ge(ada_turned, m + 1)
                nc.vector.tensor_reduce(mods[:, g, 4 * b:4 * b + 4], ps[:, bank, :].rearrange("p (c t) -> p c t", c=4),
                                        AX.X, ALU.add).then_inc(ada_reduced, 1)

            def add_bias(n, batches, g, first, last):
                dve.wait_ge(ada_reduced, batches)
                b = col(g // 3, L_ADAB, (g % 3) * 3 * KC)
                nc.vector.tensor_tensor(mods[:, g, first:last], mods[:, g, first:last], par[:, b + first:b + last],
                                        ALU.add).then_inc(mods_step, 1)
                dve.wait_ge(mods_step, n + 1)

            def finish_gate(g):
                nc.vector.tensor_scalar(gate[:, g, :], mods[:, g, 2 * KC:3 * KC], 1.0 if g % 3 == 1 else 0.5, None,
                                        ALU.mult).then_inc(gate_done, 1)

            def finish_gain(g):
                b = col(g // 3, L_NG, (g % 3) * KC)
                nc.vector.scalar_tensor_tensor(out=gs[:, g, :], in0=mods[:, g, KC:2 * KC], scalar=1.0,
                                               in1=par[:, b:b + KC], op0=ALU.add, op1=ALU.mult).then_inc(mods_done, 1)

            def hidden(f):
                nc.vector.tensor_tensor(tmp_b[:], tmp_a[:], pair(B_U), ALU.mult).then_inc(mid_done, 1)

            def ffn(f):
                base = ffn_base(f)
                n = 3 * (f // 2) + 2 * (f % 2)
                norm(n)
                if f == 0:
                    lo(1)
                lo(base + 2)
                if f == 0:
                    first_gate()
                lo(base + 3)
                dve.wait_ge(silu_done, f * FB + 1)
                dve.wait_ge(panel_done, base + 2)
                hidden(f)
                lo(base + 4)
                dve.wait_ge(mid_hi_done, f * FB + 1)
                split_lo(mid_lo[:], tmp_b[:], mid_hi[:]).then_inc(mid_lo_done, 1)
                groups = ada_groups(f)
                if f == 0:
                    for b in (4, 5):
                        reduce_turned(b, (B_ADA, B_STAT)[b % 2], 0, b)
                    add_bias(1, 6, 0, 2 * KC, 3 * KC)
                    finish_gate(0)
                if ADA_PLAN[f]:
                    dve.wait_ge(ada_step, ada_before(f))
                    dve.wait_ge(cleared, 1 + sum(len(ada_clears(e)) for e in range(f + 1)))

                def body(j, ph):
                    p = base + 2
                    units = len(ADA_PLAN[f][ph][2]) if ph is not None else 0

                    def unit(i):
                        slot, g, shift = ADA_PLAN[f][ph][2][i]
                        dve.wait_ge(ada_in[slot], j * 16 + ada_dmas(f, ph, i))
                        dve.wait_ge(ada_step, j * units + ada_free(f, ph, i))
                        nc.vector.scalar_tensor_tensor(out=ada_acc[slot], in0=ada_raw[slot],
                                                       scalar=c_act[:, bass.ds(j + shift if shift else j, 1)],
                                                       in1=ada_acc[slot], op0=ALU.mult,
                                                       op1=ALU.add).then_inc(ada_step, 1)

                    lo_loop(j, p + 3)
                    dve.wait_ge(silu_done, j + (f * FB + 2))
                    dve.wait_ge(panel_done, j * 3 + (p + 2))
                    dve.wait_ge(mid_lo_done, j + (f * FB + 1))
                    hidden(f)
                    if units == 2:
                        unit(0)
                    lo_loop(j, p + 4)
                    lo_loop(j, p + 5)
                    dve.wait_ge(mid_hi_done, j + (f * FB + 2))
                    split_lo(mid_lo[:], tmp_b[:], mid_hi[:]).then_inc(mid_lo_done, 1)
                    if units:
                        unit(units - 1)

                last = ffn_base(f) + FFN_PANELS == PANELS
                e = FB - 2
                last_unit = 0
                for ph, (first, last_unit, _) in enumerate(ADA_PLAN[f]):
                    with dve.Fori(first, last_unit) as j:
                        body(j, ph)
                if last_unit < e:
                    with dve.Fori(last_unit, e) as j:
                        body(j, None)

                def reduces(*which):
                    for i in which:
                        if i < 6 * len(groups):
                            g = groups[i // 6][0]
                            reduce_turned(ada_batches(f) + i, ADA_BANKS[i], g, i % 6)
                            if i % 6 == 5:
                                add_bias(g + 1, ada_batches(f) + i + 1, g, 0, 3 * KC)
                                finish_gain(g)
                                finish_gate(g)

                p = base + 2 + 3 * e
                reduces(0, 1)
                lo(p + 3)
                reduces(2, 3)
                dve.wait_ge(silu_done, f * FB + FB)
                dve.wait_ge(panel_done, p + 2)
                dve.wait_ge(mid_lo_done, f * FB + FB - 1)
                hidden(f)
                dve.wait_ge(mid_hi_done, f * FB + FB)
                split_lo(hB_lo[:, 0:2, :], tmp_b[:], hB_hi[:, 0:2, :]).then_inc(mid_lo_done, 1)
                reduces(4, 5)
                if not last:
                    lo(p + 4)
                reduces(6, 7)
                if not last:
                    lo(p + 5)
                reduces(8, 9, 10, 11)
                dve.wait_ge(gate_done, n + 1)
                for i in range(4):
                    if i < 3:
                        dve.wait_ge(acc_done, 3 * f + i + 1)
                    else:
                        dve.wait_ge(panel_done, base + FFN_PANELS)
                    for o in (2 * i, 2 * i + 1):
                        nc.vector.scalar_tensor_tensor(out=x[:, o, :], in0=acc(o), scalar=gate[:, n, o:o + 1],
                                                       in1=x[:, o, :], op0=ALU.mult, op1=ALU.add).then_inc(x_done, 1)

            def ada_dmas(f, ph, i):
                first, _, units = ADA_PLAN[f][ph]
                slot = units[i][0]
                n = sum(u[2] == slot for e in range(f) for u in ada_sequence(e))
                n += sum(u[2] == slot for u in ada_sequence(f) if u[0] < ph)
                return 16 * (n + 1 - first)

            def mix(l):
                base = mix_base(l)
                norm(3 * l + 1)
                lo(base + 2)
                taps_total = KC * TAPS

                def conv(first, last):
                    for s in range(first, min(last, taps_total)):
                        pr, r = divmod(s, 2 * TAPS)
                        t, c = r // 2, 2 * pr + r % 2
                        w = par[:, col(l, L_CW, c * TAPS + t):col(l, L_CW, c * TAPS + t) + 1]
                        if t == 0:
                            dve.wait_ge(glu_done, 4 * l + pr + 1)
                            b = par[:, col(l, L_CB, c):col(l, L_CB, c) + 1]
                            nc.vector.tensor_scalar(work[:, c, :], conv_in[:, c, 0:T], w, b, ALU.mult,
                                                    ALU.add).then_inc(conv_step, 1)
                        else:
                            dve.wait_ge(conv_step, taps_total * l + s - 1)
                            nc.vector.scalar_tensor_tensor(out=work[:, c, :], in0=conv_in[:, c, t:t + T], scalar=w,
                                                           in1=work[:, c, :], op0=ALU.mult,
                                                           op1=ALU.add).then_inc(conv_step, 1)
                    return min(last, taps_total)

                done = 0
                for i in range(4):
                    lo(base + 2 * i + RING)
                    if i > 0:
                        done = conv(done, done + QUOTAS[2 * i])
                    lo(base + 2 * i + 1 + RING)
                    dve.wait_ge(evac_done, 25 * l + 2 * i + 2)
                    nc.vector.tensor_tensor(conv_in[:, 2 * i:2 * i + 2, PAD:], tmp_a[:], tmp_b[:],
                                            ALU.mult).then_inc(glu_done, 1)
                    done = conv(done, done + QUOTAS[2 * i + 1])
                for i in range(M_QK, M_QK + 4):
                    lo(base + i + RING)
                    done = conv(done, done + QUOTAS[i])

                def rope_pair(g):
                    for w in range(2):
                        r = 6 * l + 2 * g + w
                        dve.wait_ge(rot_done, r + 1)
                        if r > 0:
                            dve.wait_ge(rope_done, r)
                        cos = rope_sb[:, 0:1, :].broadcast_to([P, 2, T])
                        sin = rope_sb[:, 1:2, :].broadcast_to([P, 2, T])
                        nc.vector.tensor_tensor(tmp_a[:], qk[:, g, w, :, :], cos, ALU.mult).then_inc(rope_mul, 1)
                        nc.vector.tensor_tensor(tmp_b[:], pair((2, 7)[w]), sin, ALU.mult).then_inc(rope_mul, 1)
                        dve.wait_ge(rope_mul, 2 * r + 2)
                        nc.vector.tensor_tensor(qk[:, g, w, :, :], tmp_a[:], tmp_b[:], ALU.add).then_inc(rope_done, 1)

                lo(base + M_QK + 4 + RING)
                rope_pair(0)
                done = conv(done, done + QUOTAS[12])
                lo(base + M_QK + 5 + RING)
                done = conv(done, done + QUOTAS[13])
                lo(base + M_GA0 + RING)
                rope_pair(1)
                done = conv(done, done + QUOTAS[14])
                lo(base + M_V + RING)
                rope_pair(2)
                done = conv(done, done + QUOTAS[15])

                def masked(h):
                    for q in range(TT):
                        u = 2 * h + q
                        n = 2 * HPG * l + u
                        keys = (q + 1) * P
                        dve.wait_ge(score_done, n + 1)
                        nc.vector.scalar_tensor_tensor(out=probs[q], in0=(S1 if q else S0), scalar=HD ** -0.5,
                                                       in1=mask_sb[:, q, :, 0:keys], op0=ALU.mult,
                                                       op1=ALU.add).then_inc(masked_done, 1)
                    for q in range(TT):
                        u = 2 * h + q
                        n = 2 * HPG * l + u
                        dve.wait_ge(masked_done, n + 1)
                        nc.vector.tensor_reduce(negmax[:, u:u + 1], probs[q], AX.XY, ALU.max,
                                                negate=True).then_inc(max_done, 1)

                def row_scales(h):
                    for q in range(TT):
                        u = 2 * h + q
                        dve.wait_ge(exp_done, 2 * HPG * l + u + 1)
                        nc.vector.reciprocal(rden[:, u:u + 1], den[:, u:u + 1]).then_inc(rden_done, 1)

                def head_out(c):
                    dve.wait_ge(o_hi_done, 2 * l + c + 1)
                    nc.vector.tensor_tensor(mid_lo[:, c, :], ps[:, 6 + c, 0:T], mid_hi[:, c, :].bitcast(F32),
                                            ALU.subtract).then_inc(o_lo_done, 1)

                for h in range(HPG):
                    masked(h)
                    done = conv(done, done + 4)
                    row_scales(h)
                    lo(base + M_V + 1 + 2 * h + RING)
                    if h == 2:
                        head_out(0)
                    done = conv(done, done + QUOTAS[16 + 2 * h])
                    lo(base + M_V + 2 + 2 * h + RING)
                    done = conv(done, done + QUOTAS[17 + 2 * h])
                head_out(1)
                done = conv(done, done + QUOTAS[24])
                lo(base + M_G + 6 + RING)
                conv(done, taps_total)

                dve.wait_ge(ln_sum, 2 * l + 1)
                for k in range(KC):
                    nc.vector.scalar_tensor_tensor(out=work[:, k, :], in0=ps[:, B_STAT, 0:T], scalar=-1.0 / D,
                                                   in1=work[:, k, :], op0=ALU.mult, op1=ALU.add).then_inc(xc_done, 1)
                dve.wait_ge(gates_done, 2 * l + 1)

                def gated(i):
                    if i < 3:
                        dve.wait_ge(ao_done, 3 * l + i + 1)
                    else:
                        dve.wait_ge(panel_done, base + M_AO + 1)
                    nc.vector.tensor_tensor(y_attn[:, 2 * i:2 * i + 2, :], pair(i), gates[:, 2 * i:2 * i + 2, :],
                                            ALU.mult).then_inc(ya_done, 1)

                gated(0)
                gated(1)
                recip(l, ln_std, ln_rstd)
                for k in range(KC + 2):
                    if k < KC:
                        dve.wait_ge(ln_sq, KC * (l + 1))
                        nc.vector.scalar_tensor_tensor(out=conv_in[:, k, PAD:], in0=work[:, k, :],
                                                       scalar=par[:, col(l, L_LG, k):col(l, L_LG, k) + 1], in1=rstd[:],
                                                       op0=ALU.mult, op1=ALU.mult).then_inc(ln_t, 1)
                    if k > 1:
                        dve.wait_ge(ln_hi, KC * l + k - 1)
                        split_lo(hA_lo[:, k - 2, :], work[:, k - 2, :], hA_hi[:, k - 2, :]).then_inc(ln_lo, 1)
                gated(2)
                gated(3)
                lo(base + M_AO + RING)
                for i in range(4):
                    dve.wait_ge(panel_done, base + M_CO + i + 1)
                    dve.wait_ge(gates_done, 2 * l + 2)
                    nc.vector.tensor_tensor(tmp_a[:], pair(4 + i % 2), gates[:, 8 + 2 * i:10 + 2 * i, :],
                                            ALU.mult).then_inc(yc_done, 1)
                    dve.wait_ge(yc_done, 4 * l + i + 1)
                    if i > 0:
                        dve.wait_ge(y_lo_done, 4 * l + i)
                    nc.vector.tensor_tensor(tmp_b[:], tmp_a[:], y_attn[:, 2 * i:2 * i + 2, :], ALU.add).then_inc(y_done, 1)
                    dve.wait_ge(y_hi_done, 4 * l + i + 1)
                    split_lo(hB_lo[:, 2 * i:2 * i + 2, :], tmp_b[:], hB_hi[:, 2 * i:2 * i + 2, :]).then_inc(y_lo_done, 1)
                    lo(base + M_CO + i + RING)
                g = 3 * l + 1
                dve.wait_ge(gate_done, g + 1)
                for i in range(4):
                    dve.wait_ge(panel_done, base + M_WO + i + 1)
                    for o in (2 * i, 2 * i + 1):
                        nc.vector.scalar_tensor_tensor(out=x[:, o, :], in0=pair(i)[:, o % 2, :], scalar=gate[:, g, o:o + 1],
                                                       in1=x[:, o, :], op0=ALU.mult, op1=ALU.add).then_inc(x_done, 1)
                    if i < 3:
                        lo(base + M_WO + i + RING)

            def first_unit(n, k, src, a, b):
                if n:
                    dve.wait_ge(ada_step, n)
                nc.vector.scalar_tensor_tensor(out=ada_acc[0][:, a:b], in0=src, scalar=c_act[:, k:k + 1],
                                               in1=ada_acc[0][:, a:b], op0=ALU.mult, op1=ALU.add).then_inc(ada_step, 1)

            def first_group():
                for k in range(KC):
                    dve.wait_ge(first_in[k % 4], 16 * (k // 4 + 1))
                    first_unit(k, k, first_raw[k % 4], 0, 2 * D)

            def first_gate():
                for k in range(KC):
                    if k % 2 == 0:
                        dve.wait_ge(first_in[k // 2], 16 * 3)
                    first_unit(KC + k, k, first_raw[k // 2][:, (k % 2) * D:(k % 2 + 1) * D], 2 * D, GW)

            nc.vector.memset(ones[:], 1.0).then_inc(setup_done, 1)
            nc.vector.memset(zeros[:], 0.0).then_inc(setup_done, 1)
            nc.vector.memset(eps[:], EPS).then_inc(setup_done, 1)
            nc.vector.memset(conv_in[:], 0.0).then_inc(setup_done, 1)
            dve.wait_ge(cleared, 1)
            dve.wait_ge(c_ready, 1)
            first_group()
            lo(0)
            for b in range(4):
                reduce_turned(b, (B_ADA, B_U)[b % 2], 0, b)
            add_bias(0, 4, 0, 0, 2 * KC)
            finish_gain(0)
            for l in range(DEPTH):
                ffn(2 * l)
                mix(l)
                ffn(2 * l + 1)
            norm(3 * DEPTH)


def kernel(**inputs):
    import numpy as np
    import concourse.bacc as bacc
    from concourse.bass_utils import run_bass_kernel_spmd

    def columns(a):
        a = np.asarray(a)
        n = a.shape[-1] // P
        return a.reshape(-1, n, P).transpose(2, 0, 1).reshape(P, -1)

    a = {k: np.asarray(v) for k, v in inputs.items()}
    parts = [columns(a["c"]), columns(a["final_g"])]
    for l in range(DEPTH):
        taps = a["conv_w"][l].reshape(TAPS, KC, P).transpose(2, 1, 0).reshape(P, KC * TAPS)
        parts += [columns(a["ada_b"][l]), columns(a["norm_g"][l]), taps, columns(a["conv_b"][l]),
                  columns(a["conv_ln_g"][l]), columns(a["conv_ln_b"][l])]
    params = np.concatenate(parts, axis=1)
    xT = a["x"].reshape(T, KC, P).transpose(2, 1, 0)

    import ml_dtypes
    half = HD // 2
    inv_freq = (np.float32(10000.0) ** (-(np.arange(half, dtype=np.float32) * np.float32(2.0) / np.float32(HD)))).astype(np.float32)
    ang = np.arange(T, dtype=np.float32)[None, :] * inv_freq[:, None]
    rows = np.arange(P) % half
    rope = np.stack([np.cos(ang)[rows], np.sin(ang)[rows]], axis=1).astype(np.float32)
    perm = np.zeros((P, 2, P), np.float32)
    for r in range(P):
        if r % HD < half:
            perm[r + half, 0, r] = -1.0
        else:
            perm[r - half, 0, r] = 1.0
        perm[r, 1, r] = 1.0
    mask = np.zeros((P, TT, NG, T), np.float32)
    dist = (np.arange(T).reshape(TT, P).T)[:, :, None] - np.arange(T)[None, None, :]
    for g in range(NG):
        ok = (dist >= 0) & (dist <= WINDOW[g]) & (dist % DILATION[g] == 0)
        mask[:, :, g, :] = np.where(ok, 0.0, -1e30)
    arrays = {
        "xT": xT, "params": params, "rope": rope, "perm": perm, "mask": mask.astype(ml_dtypes.bfloat16),
        "ada_w": a["ada_w"], "ffn_wg": a["ffn_wg"], "ffn_wu": a["ffn_wu"], "ffn_wd": a["ffn_wd"], "w_in": a["w_in"],
        "attn_wo": a["attn_wo"], "conv_wo": a["conv_wo"], "w_out": a["w_out"],
    }
    nc = bacc.Bacc("TRN2", target_bir_lowering=False, num_devices=1)
    arrays = {f"in_{k}": np.ascontiguousarray(v) for k, v in arrays.items()}
    args = [nc.dram_tensor(k, v.shape, mybir.dt.from_np(v.dtype), kind="ExternalInput").ap() for k, v in arrays.items()]
    out = nc.dram_tensor("out_T", (P, KC, T), F32, kind="ExternalOutput").ap()
    decoder_program(nc, *args, out)
    r = run_bass_kernel_spmd(nc, [arrays], core_ids=[0])
    got = r.results[0]["out_T"]
    return got.transpose(2, 1, 0).reshape(1, T, D)
```
